# Optimizing a Trainium2 kernel written in Bass

```python
import jax, jax.numpy as jnp
from jax import lax
import numpy as np
import math

D_MODEL = 1024
BATCH = 1
SEQ = 512
DEPTH = 1

D_MIX = D_MODEL
ATTN_HEAD_DIM = 64
ATTN_HEADS = (D_MIX // 2) // ATTN_HEAD_DIM
ATTN_KV_HEADS = 2
ATTN_WIDTH = ATTN_HEADS * ATTN_HEAD_DIM
ATTN_KV_WIDTH = ATTN_KV_HEADS * ATTN_HEAD_DIM
WINDOW = 128
BLOCK = 128
ROPE_THETA = 10000.0

GLA_HEADS = 4
GLA_WIDTH = D_MIX - ATTN_WIDTH
GLA_DV = GLA_WIDTH // GLA_HEADS
GLA_DK = GLA_DV // 2
GLA_QK_WIDTH = GLA_HEADS * GLA_DK
GLA_GATE_RANK = 16
GLA_GATE_TAU = 16.0
GLA_CHUNK = 64

D_FF = 2816
PLE_DIM = 256
EPS = 1e-6

IN_SIZES = (ATTN_WIDTH, ATTN_KV_WIDTH, ATTN_KV_WIDTH,
            GLA_QK_WIDTH, GLA_QK_WIDTH, GLA_WIDTH, GLA_GATE_RANK, GLA_WIDTH)
D_IN = sum(IN_SIZES)


def rmsnorm(x, g):
    xf = x.astype(jnp.float32)
    y = xf * lax.rsqrt(jnp.mean(xf * xf, axis=-1, keepdims=True) + EPS)
    return (y * g.astype(jnp.float32)).astype(x.dtype)

def swiglu(x, w_gate, w_up, w_down):
    return (jax.nn.silu(x @ w_gate) * (x @ w_up)) @ w_down

def rope(x, pos):
    dh = x.shape[-1]
    inv_freq = ROPE_THETA ** (-jnp.arange(0, dh, 2, dtype=jnp.float32) / dh)
    ang = pos.astype(jnp.float32)[:, None] * inv_freq[None, :]
    cos = jnp.cos(ang)[None, :, None, :]
    sin = jnp.sin(ang)[None, :, None, :]
    xf = x.astype(jnp.float32)
    x1, x2 = xf[..., : dh // 2], xf[..., dh // 2:]
    out = jnp.concatenate([x1 * cos - x2 * sin, x2 * cos + x1 * sin], axis=-1)
    return out.astype(x.dtype)

def split_cols(z):
    points = np.cumsum(IN_SIZES)[:-1].tolist()
    return jnp.split(z, points, axis=-1)

def sliding_window_attention(q, k, v, sinks):
    B, S, H, Dh = q.shape
    KVH = k.shape[2]
    G = H // KVH
    NB = S // BLOCK
    qb = q.reshape(B, NB, BLOCK, KVH, G, Dh)

    def band(t):
        tb = t.reshape(B, NB, BLOCK, KVH, Dh)
        prev = jnp.pad(tb[:, :-1], ((0, 0), (1, 0), (0, 0), (0, 0), (0, 0)))
        return jnp.concatenate([prev, tb], axis=2)

    kb, vb = band(k), band(v)
    scores = jnp.einsum('bnqhgd,bnkhd->bnhgqk', qb, kb).astype(jnp.float32) * (Dh ** -0.5)
    qi = jnp.arange(BLOCK)[:, None]
    kj = jnp.arange(2 * BLOCK)[None, :]
    rel = kj - BLOCK - qi
    in_band = (rel <= 0) & (rel > -WINDOW)
    kpos = jnp.arange(NB)[:, None, None] * BLOCK + kj[None] - BLOCK
    valid = in_band[None] & (kpos >= 0)
    scores = jnp.where(valid[None, :, None, None], scores, -jnp.inf)
    sink = sinks.astype(jnp.float32).reshape(KVH, G)[None, None, :, :, None, None]
    m = jnp.maximum(jnp.max(scores, axis=-1, keepdims=True), sink)
    e = jnp.exp(scores - m)
    denom = jnp.sum(e, axis=-1, keepdims=True) + jnp.exp(sink - m)
    probs = (e / denom).astype(v.dtype)
    out = jnp.einsum('bnhgqk,bnkhd->bnqhgd', probs, vb)
    return out.reshape(B, S, H * Dh)

def gla_chunked(q, k, v, log_alpha):
    B, S, H, DK = q.shape
    DV = v.shape[-1]
    C = GLA_CHUNK
    NC = S // C

    def chunks(t):
        return t.astype(jnp.float32).reshape(B, NC, C, H, t.shape[-1]).transpose(1, 0, 3, 2, 4)

    qc = chunks(q) * (DK ** -0.5)
    kc, vc, gc = chunks(k), chunks(v), chunks(log_alpha)
    causal = jnp.tril(jnp.ones((C, C), dtype=bool))[None, None, :, :, None]

    def step(state, inp):
        qi, ki, vi, gi = inp
        b = jnp.cumsum(gi, axis=2)
        b_last = b[:, :, -1:, :]
        diff = b[:, :, :, None, :] - b[:, :, None, :, :]
        decay = jnp.exp(jnp.where(causal, diff, -jnp.inf))
        attn = jnp.einsum('bhid,bhjd,bhijd->bhij', qi, ki, decay)
        o = (jnp.einsum('bhij,bhjv->bhiv', attn, vi)
             + jnp.einsum('bhid,bhdv->bhiv', qi * jnp.exp(b), state))
        new_state = (jnp.swapaxes(jnp.exp(b_last), 2, 3) * state
                     + jnp.einsum('bhjd,bhjv->bhdv', ki * jnp.exp(b_last - b), vi))
        return new_state, o

    s0 = jnp.zeros((B, H, DK, DV), jnp.float32)
    _, o = lax.scan(step, s0, (qc, kc, vc, gc))
    return o.transpose(1, 0, 3, 2, 4).reshape(B, S, H, DV).astype(v.dtype)

def first_inputs(seed: int = 0) -> dict:
    key = jax.random.key(seed)
    ks = jax.random.split(key, 24)
    L, D, F = DEPTH, D_MODEL, D_FF

    def w(k, shape, fan_in):
        return jax.random.normal(k, shape, jnp.float32) * (fan_in ** -0.5)

    def gain(k, shape):
        return 1.0 + 0.05 * jax.random.normal(k, shape, jnp.float32)

    return {
        "x": jax.random.normal(ks[0], (BATCH, SEQ, D), jnp.float32),
        "p": jax.random.normal(ks[1], (L, BATCH, SEQ, PLE_DIM), jnp.float32),
        "ffn1_norm": gain(ks[2], (L, D)),
        "ffn1_w_gate": w(ks[3], (L, D, F), D),
        "ffn1_w_up": w(ks[4], (L, D, F), D),
        "ffn1_w_down": w(ks[5], (L, F, D), F),
        "mix_norm": gain(ks[6], (L, D)),
        "w_in": w(ks[7], (L, D, D_IN), D),
        "q_norm": gain(ks[8], (L, ATTN_HEAD_DIM)),
        "k_norm": gain(ks[9], (L, ATTN_HEAD_DIM)),
        "attn_sinks": 0.5 * jax.random.normal(ks[10], (L, ATTN_HEADS), jnp.float32),
        "gla_w_gate_up": w(ks[11], (L, GLA_GATE_RANK, GLA_QK_WIDTH), GLA_GATE_RANK),
        "gla_b_gate": 0.1 * jax.random.normal(ks[12], (L, GLA_QK_WIDTH), jnp.float32),
        "gla_out_norm": gain(ks[13], (L, GLA_DV)),
        "w_out": w(ks[14], (L, D_MIX, D), D_MIX),
        "ffn2_norm": gain(ks[15], (L, D)),
        "ffn2_w_gate": w(ks[16], (L, D, F), D),
        "ffn2_w_up": w(ks[17], (L, D, F), D),
        "ffn2_w_down": w(ks[18], (L, F, D), F),
        "ple_gate_norm": gain(ks[19], (L, D)),
        "ple_w_gate": w(ks[20], (L, D, D), D),
        "ple_w_proj": w(ks[21], (L, PLE_DIM, D), PLE_DIM),
        "ple_norm": gain(ks[22], (L, D)),
    }

def first_block(x, p, ffn1_norm, ffn1_w_gate, ffn1_w_up, ffn1_w_down, mix_norm, w_in,
              q_norm, k_norm, attn_sinks, gla_w_gate_up, gla_b_gate, gla_out_norm, w_out,
              ffn2_norm, ffn2_w_gate, ffn2_w_up, ffn2_w_down,
              ple_gate_norm, ple_w_gate, ple_w_proj, ple_norm):
    B, S, _ = x.shape
    pos = jnp.arange(S)
    h = x
    for i in range(DEPTH):
        h = h + 0.5 * swiglu(rmsnorm(h, ffn1_norm[i]), ffn1_w_gate[i], ffn1_w_up[i], ffn1_w_down[i])

        n = rmsnorm(h, mix_norm[i])
        aq, ak, av, gq, gk, gv, glr, gog = split_cols(n @ w_in[i])

        aq = rope(rmsnorm(aq.reshape(B, S, ATTN_HEADS, ATTN_HEAD_DIM), q_norm[i]), pos)
        ak = rope(rmsnorm(ak.reshape(B, S, ATTN_KV_HEADS, ATTN_HEAD_DIM), k_norm[i]), pos)
        av = av.reshape(B, S, ATTN_KV_HEADS, ATTN_HEAD_DIM)
        attn_o = sliding_window_attention(aq, ak, av, attn_sinks[i])

        log_alpha = jax.nn.log_sigmoid(
            (glr @ gla_w_gate_up[i] + gla_b_gate[i]).astype(jnp.float32)) / GLA_GATE_TAU
        gla_o = gla_chunked(gq.reshape(B, S, GLA_HEADS, GLA_DK),
                            gk.reshape(B, S, GLA_HEADS, GLA_DK),
                            gv.reshape(B, S, GLA_HEADS, GLA_DV),
                            log_alpha.reshape(B, S, GLA_HEADS, GLA_DK))
        gla_o = rmsnorm(gla_o, gla_out_norm[i]) * jax.nn.silu(gog.reshape(B, S, GLA_HEADS, GLA_DV))
        gla_o = gla_o.reshape(B, S, GLA_WIDTH)

        h = h + jnp.concatenate([attn_o, gla_o], axis=-1) @ w_out[i]

        h = h + 0.5 * swiglu(rmsnorm(h, ffn2_norm[i]), ffn2_w_gate[i], ffn2_w_up[i], ffn2_w_down[i])

        gate = jax.nn.sigmoid(rmsnorm(h, ple_gate_norm[i]) @ ple_w_gate[i])
        emb = rmsnorm(p[i] @ ple_w_proj[i], ple_norm[i])
        h = h + gate * emb
    return h


DEPTH_2 = 2

CHUNK = 64
Q_BLOCK = 128
ROPE_THETA_2 = 500000.0
ROPE_FRACTION = 4
NORM_EPS = 1e-6
N_MIXERS = 2
DIFF_HEAD_DIM = 64
DIFF_HEADS = D_MODEL // (2 * DIFF_HEAD_DIM)
DIFF_V_DIM = 2 * DIFF_HEAD_DIM
DSA_HEAD_DIM = 64
DSA_HEADS = D_MODEL // DSA_HEAD_DIM
DSA_Q_RANK = D_MODEL // 4
IDX_HEADS = 8
IDX_DIM = 64
TOPK_MAX = 256
D_FF_2 = 4 * D_MODEL

N_DIFF_LAYERS = (DEPTH_2 + 1) // 2
N_DSA_LAYERS = DEPTH_2 // 2


def rms_norm(x, g=None):
    xf = x.astype(jnp.float32)
    y = xf * lax.rsqrt(jnp.mean(xf * xf, axis=-1, keepdims=True) + NORM_EPS)
    if g is not None:
        y = y * g.astype(jnp.float32)
    return y.astype(x.dtype)

def rope_tables(positions, head_dim):
    rot = head_dim // ROPE_FRACTION
    inv = ROPE_THETA_2 ** (-jnp.arange(0, rot, 2, dtype=jnp.float32) / rot)
    ang = positions.astype(jnp.float32)[..., None] * inv
    return jnp.cos(ang)[:, :, None, :], jnp.sin(ang)[:, :, None, :]

def apply_partial_rope(x, cos, sin):
    half = cos.shape[-1]
    rot = 2 * half
    x1 = x[..., :half].astype(jnp.float32)
    x2 = x[..., half:rot].astype(jnp.float32)
    r = jnp.concatenate([x1 * cos - x2 * sin, x2 * cos + x1 * sin], axis=-1).astype(x.dtype)
    return jnp.concatenate([r, x[..., rot:]], axis=-1)

def diff_attention(h, w_in, q_g, k_g, lam_q1, lam_k1, lam_q2, lam_k2, subln_g, w_out,
                   cos, sin, lam_init):
    B, S, _ = h.shape
    H, d = DIFF_HEADS, DIFF_HEAD_DIM
    proj = h @ w_in
    q, k, v = jnp.split(proj, [2 * H * d, 4 * H * d], axis=-1)
    q = apply_partial_rope(rms_norm(q.reshape(B, S, 2 * H, d), q_g), cos, sin) * (d ** -0.5)
    k = apply_partial_rope(rms_norm(k.reshape(B, S, 2 * H, d), k_g), cos, sin)
    q = q.reshape(B, S, H, 2, d)
    k = k.reshape(B, S, H, 2, d)
    v = v.reshape(B, S, H, DIFF_V_DIM)
    lam = (jnp.exp(jnp.sum(lam_q1.astype(jnp.float32) * lam_k1.astype(jnp.float32)))
           - jnp.exp(jnp.sum(lam_q2.astype(jnp.float32) * lam_k2.astype(jnp.float32)))
           + lam_init)
    n_blocks = S // Q_BLOCK
    key_chunk = jnp.arange(S) // CHUNK
    q_blocks = q.reshape(B, n_blocks, Q_BLOCK, H, 2, d).swapaxes(0, 1)

    def block(args):
        qb, start = args
        q_chunk = (start + jnp.arange(Q_BLOCK)) // CHUNK
        mask = key_chunk[None, :] <= q_chunk[:, None]
        s = jnp.einsum('bqhcd,bkhcd->bhcqk', qb, k).astype(jnp.float32)
        p = jax.nn.softmax(jnp.where(mask, s, -jnp.inf), axis=-1)
        a = p[:, :, 0] - lam * p[:, :, 1]
        return jnp.einsum('bhqk,bkhe->bqhe', a.astype(v.dtype), v)

    o = lax.map(block, (q_blocks, jnp.arange(n_blocks) * Q_BLOCK))
    o = o.swapaxes(0, 1).reshape(B, S, H, DIFF_V_DIM)
    o = rms_norm(o, subln_g) * (1.0 - lam_init)
    return o.reshape(B, S, H * DIFF_V_DIM) @ w_out

def dsa_attention(h, w_in, cq_g, w_uq, w_uq_idx, q_g, k_g, w_out, cos, sin):
    B, S, _ = h.shape
    H, d, R, HI, DI = DSA_HEADS, DSA_HEAD_DIM, DSA_Q_RANK, IDX_HEADS, IDX_DIM
    proj = h @ w_in
    c_q, k, v, k_idx, w_idx = jnp.split(
        proj, [R, R + H * d, R + 2 * H * d, R + 2 * H * d + DI], axis=-1)
    c_q = rms_norm(c_q, cq_g)
    q = (c_q @ w_uq).reshape(B, S, H, d)
    q_idx = apply_partial_rope((c_q @ w_uq_idx).reshape(B, S, HI, DI), cos, sin)
    k_idx = apply_partial_rope(rms_norm(k_idx)[:, :, None, :], cos, sin)[:, :, 0]
    w_idx = w_idx * ((HI ** -0.5) * (DI ** -0.5))
    q = apply_partial_rope(rms_norm(q, q_g), cos, sin) * (d ** -0.5)
    k = apply_partial_rope(rms_norm(k.reshape(B, S, H, d), k_g), cos, sin)
    v = v.reshape(B, S, H, d)
    topk = min(TOPK_MAX, S // 4)
    n_blocks = S // Q_BLOCK
    key_chunk = jnp.arange(S) // CHUNK
    qb_all = q.reshape(B, n_blocks, Q_BLOCK, H, d).swapaxes(0, 1)
    qib_all = q_idx.reshape(B, n_blocks, Q_BLOCK, HI, DI).swapaxes(0, 1)
    wb_all = w_idx.reshape(B, n_blocks, Q_BLOCK, HI).swapaxes(0, 1)
    gather = jax.vmap(lambda arr, ids: arr[ids])

    def block(args):
        qb, qib, wb, start = args
        q_chunk = (start + jnp.arange(Q_BLOCK)) // CHUNK
        mask = key_chunk[None, :] <= q_chunk[:, None]
        dots = jnp.einsum('bqhe,bke->bqhk', qib, k_idx).astype(jnp.float32)
        score = jnp.einsum('bqh,bqhk->bqk', wb.astype(jnp.float32), jax.nn.relu(dots))
        score = jnp.where(mask, score, -jnp.inf)
        vals, idx = lax.top_k(score, topk)
        valid = jnp.isfinite(vals)
        kg = gather(k, idx)
        vg = gather(v, idx)
        s = jnp.einsum('bqhd,bqkhd->bhqk', qb, kg).astype(jnp.float32)
        p = jax.nn.softmax(jnp.where(valid[:, None], s, -jnp.inf), axis=-1)
        return jnp.einsum('bhqk,bqkhd->bqhd', p.astype(vg.dtype), vg)

    o = lax.map(block, (qb_all, qib_all, wb_all, jnp.arange(n_blocks) * Q_BLOCK))
    o = o.swapaxes(0, 1).reshape(B, S, H * d)
    return o @ w_out

def sq_relu_mlp(h, w1, w2):
    u = jax.nn.relu(h @ w1)
    return (u * u) @ w2

def second_inputs(seed: int = 0) -> dict:
    key = jax.random.key(seed)
    ks = iter(jax.random.split(key, 32))
    D = D_MODEL

    def nrm(shape, scale):
        return jax.random.normal(next(ks), shape, jnp.float32) * scale

    def gain(shape):
        return 1.0 + nrm(shape, 0.02)

    nA, nB = N_DIFF_LAYERS, N_DSA_LAYERS
    dsa_in = DSA_Q_RANK + 2 * DSA_HEADS * DSA_HEAD_DIM + IDX_DIM + IDX_HEADS
    x = nrm((BATCH, SEQ, D), 1.0)
    offset = jax.random.randint(next(ks), (BATCH, 1), 0, 4096, dtype=jnp.int32)
    positions = (offset + jnp.arange(SEQ, dtype=jnp.int32)[None, :]).astype(jnp.int32)
    return {
        "x": x,
        "positions": positions,
        "norm_mix": gain((DEPTH_2, D)),
        "norm_mlp": gain((DEPTH_2, D)),
        "mlp_w1": nrm((DEPTH_2, D, D_FF_2), D ** -0.5),
        "mlp_w2": nrm((DEPTH_2, D_FF_2, D), D_FF_2 ** -0.5),
        "diff_w_in": nrm((nA, D, 6 * DIFF_HEADS * DIFF_HEAD_DIM), D ** -0.5),
        "diff_q_norm": gain((nA, DIFF_HEAD_DIM)),
        "diff_k_norm": gain((nA, DIFF_HEAD_DIM)),
        "diff_lam_q1": nrm((nA, DIFF_HEAD_DIM), 0.1),
        "diff_lam_k1": nrm((nA, DIFF_HEAD_DIM), 0.1),
        "diff_lam_q2": nrm((nA, DIFF_HEAD_DIM), 0.1),
        "diff_lam_k2": nrm((nA, DIFF_HEAD_DIM), 0.1),
        "diff_subln": gain((nA, DIFF_V_DIM)),
        "diff_w_out": nrm((nA, DIFF_HEADS * DIFF_V_DIM, D), (DIFF_HEADS * DIFF_V_DIM) ** -0.5),
        "dsa_w_in": nrm((nB, D, dsa_in), D ** -0.5),
        "dsa_cq_norm": gain((nB, DSA_Q_RANK)),
        "dsa_w_uq": nrm((nB, DSA_Q_RANK, DSA_HEADS * DSA_HEAD_DIM), DSA_Q_RANK ** -0.5),
        "dsa_w_uq_idx": nrm((nB, DSA_Q_RANK, IDX_HEADS * IDX_DIM), DSA_Q_RANK ** -0.5),
        "dsa_q_norm": gain((nB, DSA_HEAD_DIM)),
        "dsa_k_norm": gain((nB, DSA_HEAD_DIM)),
        "dsa_w_out": nrm((nB, DSA_HEADS * DSA_HEAD_DIM, D), (DSA_HEADS * DSA_HEAD_DIM) ** -0.5),
    }

def second_block(x, positions, norm_mix, norm_mlp, mlp_w1, mlp_w2,
              diff_w_in, diff_q_norm, diff_k_norm, diff_lam_q1, diff_lam_k1,
              diff_lam_q2, diff_lam_k2, diff_subln, diff_w_out,
              dsa_w_in, dsa_cq_norm, dsa_w_uq, dsa_w_uq_idx, dsa_q_norm, dsa_k_norm,
              dsa_w_out):
    cos, sin = rope_tables(positions, DIFF_HEAD_DIM)
    for i in range(DEPTH_2):
        h = rms_norm(x, norm_mix[i])
        j = i // N_MIXERS
        if i % N_MIXERS == 0:
            lam_init = 0.8 - 0.6 * math.exp(-0.3 * i)
            mix = diff_attention(h, diff_w_in[j], diff_q_norm[j], diff_k_norm[j],
                                 diff_lam_q1[j], diff_lam_k1[j], diff_lam_q2[j],
                                 diff_lam_k2[j], diff_subln[j], diff_w_out[j],
                                 cos, sin, lam_init)
        else:
            mix = dsa_attention(h, dsa_w_in[j], dsa_cq_norm[j], dsa_w_uq[j],
                                dsa_w_uq_idx[j], dsa_q_norm[j], dsa_k_norm[j],
                                dsa_w_out[j], cos, sin)
        x = x + mix
        x = x + sq_relu_mlp(rms_norm(x, norm_mlp[i]), mlp_w1[i], mlp_w2[i])
    return x


def setup_inputs(seed=0):
    out = dict(first_inputs(seed))
    for name, value in second_inputs(seed + 1).items():
        if name != "x":
            out[name + "_2"] = value
    return out


def reference(
    x, p, ffn1_norm, ffn1_w_gate, ffn1_w_up, ffn1_w_down, mix_norm, w_in, q_norm, k_norm,
    attn_sinks, gla_w_gate_up, gla_b_gate, gla_out_norm, w_out, ffn2_norm, ffn2_w_gate,
    ffn2_w_up, ffn2_w_down, ple_gate_norm, ple_w_gate, ple_w_proj, ple_norm, positions_2,
    norm_mix_2, norm_mlp_2, mlp_w1_2, mlp_w2_2, diff_w_in_2, diff_q_norm_2, diff_k_norm_2,
    diff_lam_q1_2, diff_lam_k1_2, diff_lam_q2_2, diff_lam_k2_2, diff_subln_2, diff_w_out_2,
    dsa_w_in_2, dsa_cq_norm_2, dsa_w_uq_2, dsa_w_uq_idx_2, dsa_q_norm_2, dsa_k_norm_2,
    dsa_w_out_2,
):
    x = first_block(
        x, p, ffn1_norm, ffn1_w_gate, ffn1_w_up, ffn1_w_down, mix_norm, w_in, q_norm, k_norm,
        attn_sinks, gla_w_gate_up, gla_b_gate, gla_out_norm, w_out, ffn2_norm, ffn2_w_gate,
        ffn2_w_up, ffn2_w_down, ple_gate_norm, ple_w_gate, ple_w_proj, ple_norm,
    )
    return second_block(
        x, positions_2, norm_mix_2, norm_mlp_2, mlp_w1_2, mlp_w2_2, diff_w_in_2, diff_q_norm_2,
        diff_k_norm_2, diff_lam_q1_2, diff_lam_k1_2, diff_lam_q2_2, diff_lam_k2_2, diff_subln_2,
        diff_w_out_2, dsa_w_in_2, dsa_cq_norm_2, dsa_w_uq_2, dsa_w_uq_idx_2, dsa_q_norm_2,
        dsa_k_norm_2, dsa_w_out_2,
    )


_drawn_inputs = setup_inputs


def setup_inputs(seed=0):
    import zlib

    import numpy as np

    out = dict(_drawn_inputs(seed))
    spreads = {}
    factors = {'q_norm': 7.131,
     'k_norm': 6.378,
     'attn_sinks': 7.237,
     'gla_b_gate': 2.745,
     'ple_gate_norm': 4.716,
     'norm_mix_2': 2.681,
     'norm_mlp_2': 2.733,
     'diff_q_norm_2': 5.074,
     'diff_k_norm_2': 5.011,
     'diff_lam_k1_2': 6.801,
     'diff_subln_2': 4.07,
     'dsa_cq_norm_2': 7.723,
     'dsa_q_norm_2': 8.0,
     'dsa_k_norm_2': 8.0}
    for name, (base, spread) in spreads.items():
        noise = np.random.default_rng([zlib.crc32(name.encode()), seed]).standard_normal(out[name].shape)
        drawn = base * np.exp(spread * noise) if base else spread * noise
        out[name] = __import__('jax').numpy.asarray(drawn.astype(out[name].dtype))
    for name, factor in factors.items():
        out[name] = (out[name] * factor).astype(out[name].dtype)
    return out
```

```python
from contextlib import ExitStack
import math

import numpy as np
import concourse.bass as bass
from concourse import mybir

F32 = mybir.dt.float32
F32R = mybir.dt.float32r
BF16 = mybir.dt.bfloat16
I32 = mybir.dt.int32
U8 = mybir.dt.uint8
ALU = mybir.AluOpType
ACT = mybir.ActivationFunctionType
AX = mybir.AxisListType

P = 128
D = 1024
S = 512
KT = D // P
NT = S // P
BC = 256
EPS = 1e-6
BIG = 1e30
HD = 64
F1 = 2816
F2 = 4096
GROUPS1 = [8, 8, 6]
GROUPS2 = [8, 8, 8, 8]
TOPK = 128
LAM_INIT = 0.8 - 0.6 * math.exp(0.0)
LEVELS = [64, 32, 16, 8, 4, 2, 1]
TWO_PI = 2 * math.pi
ROUND = 1.5 * 2.0 ** 23

G_FFN1, G_MIX, G_FFN2, G_PLEG, G_PLE, G_MIX0, G_MLP0, G_MIX1, G_MLP1 = range(0, 72, 8)
G_QN, G_KN, G_GLA, G_DQ, G_DK, G_SUB, G_SQ, G_SK, G_CQ, G_BG, G_LQ, G_LK, G_SINK = (
    72, 73, 74, 75, 76, 77, 78, 79, 80, 82, 84, 85, 86)
G_ROWS = 87
NORM_GAIN = [G_FFN1, G_MIX, G_FFN2, G_PLEG, G_MIX0, G_MLP0, G_MIX1, G_MLP1]


def constants():
    c = {}
    p = np.arange(P)
    c["c_ident"] = np.eye(P, dtype=np.float32)
    sel = np.zeros((P, 2 * KT + 2, 16), np.float32)
    for t in range(KT):
        sel[p, t, 2 * t + p // HD] = 1 / HD
        sel[:, KT + t, 2 * t:2 * t + 2] = 1 / P
    sel[:, 2 * KT:, 0:4] = 1 / 256
    c["c_sel"] = sel.reshape(P, -1)
    spread = np.zeros((16, KT * P), np.float32)
    spread[np.arange(KT * P) // HD, np.arange(KT * P)] = 1
    c["c_spread"] = spread
    rot1 = np.zeros((P, P), np.float32)
    rot2 = np.zeros((P, P), np.float32)
    for h0 in (0, HD):
        for rot, half in ((rot1, 32), (rot2, 8)):
            for i in range(half):
                rot[h0 + half + i, h0 + i] = -1
                rot[h0 + i, h0 + half + i] = 1
    c["c_rot"] = np.concatenate([rot1, rot2], 1)
    d = p % HD
    inv1 = np.power(np.float32(10000.0), -(2 * (d % 32)).astype(np.float32) / np.float32(64))
    inv2 = np.where(d < 16, np.power(np.float32(500000.0), -(2 * (d % 8)).astype(np.float32) / np.float32(16)), 0)
    c["c_inv"] = np.stack([inv1, inv2], 1).astype(np.float32)
    c["c_pos"] = np.arange(S, dtype=np.float32)[None]
    qi, kj = p[:, None], np.arange(2 * P)[None]
    rel = kj - P - qi
    band = np.where((rel <= 0) & (rel > -P), 0, -BIG).astype(np.float32)
    first = np.where(kj < P, -BIG, band).astype(np.float32)
    chunk = np.where((qi < 64) & (np.arange(P)[None] >= 64), -BIG, 0).astype(np.float32)
    c["c_mask"] = np.concatenate([band, first, chunk], 1)
    j, i = p[:, None], p[None]
    lev = [((i // s) % 2 == 1) & ((j // s) % 2 == 0) & (i // (2 * s) == j // (2 * s)) for s in LEVELS]
    lev.append(i == j)
    c["c_level"] = np.stack(lev, 1).astype(np.float32).reshape(P, -1)
    half = np.zeros((P, 2, P), np.float32)
    half[:64, 0] = 1
    half[64:, 1] = 1
    c["c_half"] = half.reshape(P, -1)
    return c


def plan():
    at, n = {}, 0
    for name, groups, per in (("ffn1", GROUPS1, 2), ("mix", None, 10), ("wout1", None, 4), ("ffn2", GROUPS1, 2),
                              ("proj", None, 4), ("gate", None, 4), ("diff", None, 12), ("wout2", None, 4),
                              ("mlp0", GROUPS2, 1), ("dsa", None, 10), ("uq", None, 6), ("wout3", None, 4),
                              ("mlp1", GROUPS2, 1)):
        if groups is None:
            at[name] = n
            n += per
        else:
            for g, tiles in enumerate(groups):
                at[name, g, "up"] = n
                n += per * tiles // 2
                at[name, g, "down"] = n
                n += 4
    at["end"] = n
    return at


def program(nc, io, out):
    at = plan()
    NB = at["end"]
    ctx = ExitStack()
    with ctx:
        def sb(name, shape, dt=F32):
            return ctx.enter_context(nc.sbuf_tensor(name, shape, dt))

        sems = {}

        def sem(name):
            if name not in sems:
                sems[name] = ctx.enter_context(nc.semaphore(name))
            return sems[name]

        x_res = sb("x_res", [P, KT, S])
        w_raw = sb("w_raw", [P, 2, KT * BC])
        w_hi = sb("w_hi", [P, 2, KT * BC], F32R)
        w_lo = sb("w_lo", [P, 2, KT * BC], F32R)
        base = nc.sbuf_base() if callable(nc.sbuf_base) else nc.sbuf_base
        region = sb("region", [P, 4 * KT, S])
        region_at = base
        KB = KT * S * 4

        def alias(name, shape, dt, offset):
            return nc.alloc_sbuf_tensor_at(name, shape, dt, offset=region_at + offset)

        xg_hi = alias("xg_hi", [P, KT, S], F32R, 0)
        xg_lo = alias("xg_lo", [P, KT, S], F32R, KB)
        h_hi = alias("h_hi", [P, KT, S], F32R, 2 * KB)
        h_lo = alias("h_lo", [P, KT, S], F32R, 3 * KB)
        free_x = alias("free_x", [P, 2 * KT, S], F32, 0)
        kmask = alias("kmask", [P, NT - 1, S], BF16, 12 * S * 4)
        free_h = alias("free_h", [P, 2 * KT, S], F32, 2 * KB)

        level = alias("level", [P, 8, P], U8, 2 * KB + 14 * S * 4)
        wgu = alias("wgu", [16, 256], F32, 2 * KB + 15 * S * 4)

        rstd = sb("rstd", [P, S])
        rstd_tok = sb("rstd_tok", [P, NT])
        buf_a = sb("buf_a", [P, 2, S])
        buf_b = sb("buf_b", [P, 2, S])
        buf_c = sb("buf_c", [P, 2, S])
        buf_d = sb("buf_d", [P, 2, S])
        sq = sb("sq", [P, 2, S])
        ssq = sb("ssq", [P, S])
        cos_t = sb("cos_t", [P, S])
        sin_t = sb("sin_t", [P, S])
        arena = sb("arena", [P, 10752])
        gains = sb("gains", [P, G_ROWS])
        gcol = sb("gcol", [P, 8])
        ident = sb("ident", [P, P])
        ident_bf = sb("ident_bf", [P, P], BF16)
        sel = sb("sel", [P, 2 * KT + 2, 16])
        spread = sb("spread", [16, KT * P])
        rot = sb("rot", [P, 2, P])
        inv = sb("inv", [P, 2])
        mask_bf = sb("mask_bf", [P, 5 * P], BF16)
        mean = sb("mean", [P, P])
        eps = sb("eps", [P, 1])
        one = sb("one", [P, 1])
        sm = sb("sm", [P, 96])

        psum = ctx.enter_context(nc.psum_tensor("psum", [P, 8, S], F32))
        bank = [psum[:, i, :] for i in range(8)]

        TILES = {"gq": 5, "gla": 4, "dq": 16, "sub": 8, "cq": 2, "kx": 1, "qi": 4, "sq": 16}
        ROPE, SPLIT, NORM = ("gq", "dq", "kx", "qi", "sq"), ("gla", "sub", "cq"), tuple(t for t in TILES if t != "qi")

        def use(name, kind, v=0):
            if name in ("a2", "a3"):
                per = {"_oc": KT, "_hi": 0}.get(kind, KT * NT)
                return sem("pairs" + kind), v + (per if name == "a3" else 0)
            users = (NORM if kind in ("_sq", "_msq", "_bc", "_nrm", "_rms", "_rs") else
                     ROPE if kind in ("_rot", "_sin", "_cos") else
                     SPLIT if kind == "_hi" else ("gla",) if kind == "_pre" else tuple(TILES))
            each = (lambda n: 1) if kind in ("_rms", "_rs") else TILES.get
            return sem("norm" + kind), v + sum(each(n) for n in users[:users.index(name)])

        def rows(w, k0, nk):
            return w[P * k0:P * (k0 + nk), :].rearrange("(k p) f -> p k f", p=P)

        def wait_lo(e, c, j=0):
            e.wait_ge(sem("lo_done"), 2 * j + (c + 1))

        def load(e, c, j, src, nk=KT, cols=BC):
            if c >= 2 or not isinstance(j, int):
                e.wait_ge(sem("lo_done"), 2 * j + (c - 1))
            dst = w_raw[:, c % 2, :].rearrange("p (k f) -> p k f", f=BC)[:, 0:nk, 0:cols]
            e.dma_start(dst, src).then_inc(sem(f"landed{c % 2}"), 16)

        def hi(e, c, j=0):
            if c >= NB:
                return
            e.wait_ge(sem(f"landed{c % 2}"), 16 * j + 16 * (c // 2 + 1))
            if c >= 2:
                e.wait_ge(sem("pe_blk"), 2 * j + (c - 1))
            e.activation(w_hi[:, c % 2, :], w_raw[:, c % 2, :], ACT.Copy).then_inc(sem("hi_done"), 1)

        def lo(e, c, j=0):
            if c >= NB:
                return
            e.wait_ge(sem("hi_done"), 2 * j + (c + 1))
            e.tensor_tensor(w_lo[:, c % 2, :], w_raw[:, c % 2, :], w_hi[:, c % 2, :].bitcast(F32),
                            ALU.subtract).then_inc(sem("lo_done"), 1)

        def two(c, m):
            return bank[2 * (c % 2) + m]

        block = ctx.enter_context(nc.Block())

        @block.sync
        def _(sp):
            tok = io["x"].rearrange("a (n p) d -> p (a n) d", p=P)
            xin = arena[:, 0:4096].rearrange("p (n d) -> p n d", n=NT)
            stack = buf_d[:, 0, 0:P]
            sp.wait_ge(sem("zeroed"), 1)
            n_rows = 0

            def row(r, src):
                nonlocal n_rows
                n_rows += 1
                sp.dma_start(stack[r:r + src.shape[0], 0:src.shape[1]], src).then_inc(sem("gain_rows"), 16)

            def as_rows(v):
                return v.rearrange("a (k p) -> (a k) p", p=P)

            row(G_FFN1, as_rows(io["ffn1_norm"]))
            sp.dma_start(ident[:], io["c_ident"]).then_inc(sem("const_a"), 16)
            for n in range(NT):
                sp.dma_start(xin[:, n, :], tok[:, n, :]).then_inc(sem("x_in"), 16)
            for g, name in ((G_MIX, "mix_norm"), (G_FFN2, "ffn2_norm"), (G_PLEG, "ple_gate_norm"), (G_PLE, "ple_norm"),
                            (G_GLA, "gla_out_norm"), (G_SUB, "diff_subln_2"), (G_CQ, "dsa_cq_norm_2"), (G_BG, "gla_b_gate")):
                row(g, as_rows(io[name]))
            for i, (ga, gb) in enumerate(((G_MIX0, G_MLP0), (G_MIX1, G_MLP1))):
                row(ga, as_rows(io["norm_mix_2"][i:i + 1, :]))
                row(gb, as_rows(io["norm_mlp_2"][i:i + 1, :]))
            for g, name in ((G_QN, "q_norm"), (G_KN, "k_norm"), (G_DQ, "diff_q_norm_2"), (G_DK, "diff_k_norm_2"),
                            (G_SQ, "dsa_q_norm_2"), (G_SK, "dsa_k_norm_2")):
                for half in range(2):
                    n_rows += 1
                    sp.dma_start(stack[g:g + 1, HD * half:HD * half + HD], io[name]).then_inc(sem("gain_rows"), 16)
            for g, names in ((G_LQ, ("diff_lam_q1_2", "diff_lam_q2_2")), (G_LK, ("diff_lam_k1_2", "diff_lam_k2_2"))):
                for half in range(2):
                    n_rows += 1
                    sp.dma_start(stack[g:g + 1, HD * half:HD * half + HD], io[names[half]]).then_inc(sem("gain_rows"), 16)
            row(G_SINK, io["attn_sinks"])
            assert n_rows == 30
            load(sp, 0, 0, rows(io["ffn1_w_gate"][0], 0, KT)[:, :, 0:BC])
            load(sp, 1, 0, rows(io["ffn1_w_up"][0], 0, KT)[:, :, 0:BC])
            sp.dma_start(sel[:].rearrange("p t c -> p (t c)"), io["c_sel"]).then_inc(sem("const_b"), 16)
            sp.dma_start(spread[:], io["c_spread"]).then_inc(sem("const_b"), 16)
            sp.dma_start(rot[:].rearrange("p a c -> p (a c)"), io["c_rot"]).then_inc(sem("const_b"), 16)
            sp.dma_start(inv[:], io["c_inv"]).then_inc(sem("const_b"), 16)
            sp.wait_ge(sem("x_copied"), KT)
            sp.dma_start(arena[:, 0:5 * P], io["c_mask"]).then_inc(sem("const_c"), 16)
            sp.dma_start(arena[0:1, 1024:1536], io["c_pos"]).then_inc(sem("const_c"), 16)
            sp.dma_start(arena[:, 2048:2304], io["c_half"]).then_inc(sem("const_c"), 16)

            def ffn(name, groups, wg, wu, wd, skip=0):
                f0 = 0
                for g, tiles in enumerate(groups):
                    c = at[name, g, "up"]
                    if wg is not None:
                        vg, vu = rows(wg, 0, KT), rows(wu, 0, KT)
                        with sp.Fori(1 if g == 0 and skip else 0, tiles // 2) as j:
                            load(sp, c, j, vg[:, :, bass.ds(j * BC + P * f0, BC)])
                            load(sp, c + 1, j, vu[:, :, bass.ds(j * BC + P * f0, BC)])
                    else:
                        vu = rows(wu, 0, KT)
                        with sp.Fori(0, tiles // 4) as j:
                            for s in range(2):
                                load(sp, c + s, j, vu[:, :, bass.ds(j * 2 * BC + (P * f0 + s * BC), BC)])
                    c = at[name, g, "down"]
                    vd = rows(wd, f0, tiles)
                    with sp.Fori(0, 2) as j:
                        for s in range(2):
                            load(sp, c + s, j, vd[:, :, bass.ds(j * 2 * BC + s * BC, BC)], nk=tiles)
                    f0 += tiles

            ffn("ffn1", GROUPS1, io["ffn1_w_gate"][0], io["ffn1_w_up"][0], io["ffn1_w_down"][0], skip=1)
            c, v = at["mix"], rows(io["w_in"][0], 0, KT)
            for i, (f0, cols) in enumerate(((0, 256), (256, 256), (512, 256), (768, 256), (1024, 256), (1280, 256),
                                            (1536, 256), (1792, 16), (1808, 256), (2064, 256))):
                load(sp, c + i, 0, v[:, :, f0:f0 + cols], cols=cols)

            def plain(name, w, nblocks, nk=KT, off=0, first=0):
                c, v = at[name] + off, rows(w, 0, nk)
                for i in range(first, nblocks):
                    load(sp, c + i, 0, v[:, :, i * BC:(i + 1) * BC], nk=nk)

            plain("wout1", io["w_out"][0], 2)
            sp.wait_ge(sem("pe_blk"), at["mix"])
            sp.dma_start(free_h[:, 12:14, :].rearrange("p a c -> p (a c)"), io["c_level"]).then_inc(sem("mix_const"), 16)
            sp.dma_start(wgu[:], io["gla_w_gate_up"][0]).then_inc(sem("mix_const"), 16)
            kk, kswap = arena[:, 2048:2560], arena[:, 2560:3072]
            sp.wait_ge(*use("gq", "_out", 5))
            sp.dma_start(kswap[0:HD, :], kk[HD:P, :]).then_inc(sem("kswap"), 16)
            sp.dma_start(kswap[HD:P, :], kk[0:HD, :]).then_inc(sem("kswap"), 16)
            plain("wout1", io["w_out"][0], 4, first=2)
            sp.wait_ge(sem("pe_blk"), at["wout1"] + 1)
            sp.dma_start(arena[:, 0:1024].rearrange("p (n d) -> p n d", n=NT),
                         io["p"].rearrange("l a (n p) d -> p (l a n) d", p=P)).then_inc(sem("p_in"), 16)
            sp.dma_start(arena[0:1, 1024:1536].bitcast(I32), io["positions_2"]).then_inc(sem("p_in"), 16)
            ffn("ffn2", GROUPS1, io["ffn2_w_gate"][0], io["ffn2_w_up"][0], io["ffn2_w_down"][0])
            plain("proj", io["ple_w_proj"][0], 4, nk=2)
            plain("gate", io["ple_w_gate"][0], 4)
            plain("diff", io["diff_w_in_2"][0], 12)
            plain("wout2", io["diff_w_out_2"][0], 4)
            ffn("mlp0", GROUPS2, None, io["mlp_w1_2"][0], io["mlp_w2_2"][0])
            c, v = at["dsa"], rows(io["dsa_w_in_2"][0], 0, KT)
            load(sp, c, 0, v[:, :, 0:256])
            load(sp, c + 1, 0, v[:, :, 2304:2376], cols=72)
            for i in range(8):
                load(sp, c + 2 + i, 0, v[:, :, 256 + i * BC:512 + i * BC])
            plain("uq", io["dsa_w_uq_2"][0], 4, nk=2)
            plain("uq", io["dsa_w_uq_idx_2"][0], 2, nk=2, off=4)
            ki = arena[:, 8192 + 2048:8192 + 2560]
            plain("wout3", io["dsa_w_out_2"][0], 2)
            sp.wait_ge(*use("kx", "_out", 1))
            sp.dma_start(ki[HD:P, :], ki[0:HD, :]).then_inc(sem("kswap"), 16)
            plain("wout3", io["dsa_w_out_2"][0], 4, first=2)
            ffn("mlp1", GROUPS2, None, io["mlp_w1_2"][1], io["mlp_w2_2"][1])
            tok_out = out.rearrange("a (n p) d -> p (a n) d", p=P)
            y = arena[:, 0:4096].rearrange("p (n d) -> p n d", n=NT)
            for n in range(NT):
                sp.wait_ge(sem("y_copied"), 2 * (n + 1))
                sp.dma_start(tok_out[:, n, :], y[:, n, :]).then_inc(sem("stored"), 16)
            sp.wait_ge(sem("stored"), 16 * NT)


        rs16 = [ssq[0:16, :], rstd[0:16, :]]
        aq = arena[:, 0:2048].rearrange("p (k t) -> p k t", t=S)
        ak = arena[:, 2048:2560]
        ak_swap = arena[:, 2560:3072]
        av = arena[:, 3072:3584].rearrange("p (n f) -> p n f", n=NT)
        gq = arena[:, 3584:4608].rearrange("p (k t) -> p k t", t=S)
        gk = arena[:, 4608:5632].rearrange("p (k t) -> p k t", t=S)
        gv = arena[:, 5632:7680].rearrange("p (n f) -> p n f", n=NT)
        gog = arena[:, 7680:9728].rearrange("p (k t) -> p k t", t=S)
        cum = arena[:, 9728:10752]
        glr = ssq[0:16, :]
        emb = arena[:, 1536:5632].rearrange("p (k t) -> p k t", t=S)
        sig = arena[:, 5632:9728].rearrange("p (k t) -> p k t", t=S)
        k2 = arena[:, 0:4096].rearrange("p (k t) -> p k t", t=S)
        v2 = arena[:, 4096:8192].rearrange("p (n f) -> p n f", n=NT)
        q2 = free_h[:, 0:KT, :]
        qi = arena[:, 8192:10240].rearrange("p (k t) -> p k t", t=S)
        ki = arena[:, 10240:10752]
        cq_hi, cq_lo = h_lo[:, 0:2, :], h_lo[:, 2:4, :]
        cq = free_h[:, 12:14, :]
        kw = free_h[:, 14, :]
        acc_at = free_x[:, 0:4, :].rearrange("p h (t i) -> p h t i", i=P)
        cross_at = free_x[:, 4:10, :].rearrange("p a (b i) -> p (a b) i", i=P)
        gkx = free_x[:, 14:16, :]
        gla_o = free_x[:, 10:14, :]
        ql = [buf_a[:, :, :], free_x[:, 10:12, :]]
        kl = [buf_b[:, :, :], free_x[:, 12:14, :]]
        dl = [buf_c[:, :, :], buf_d[:, :, :]]
        band_mask, first_mask, chunk_mask = mask_bf[:, 0:256], mask_bf[:, 256:512], mask_bf[:, 512:640]
        widx = sm[:, 32:64].rearrange("p (n h) -> p n h", n=NT)
        sinks = sm[:, 88:96]
        top8 = sm[:, 80:88]
        GN = {
            "gq": dict(tiles=[(aq[:, t, :], aq[:, t, :], 0, t, gcol[:, 0:1]) for t in range(4)]
                       + [(ak, ak, 1, 0, gains[:, G_KN:G_KN + 1])], sel=0, sizes=[4, 1]),
            "dq": dict(tiles=[(q2[:, t, :], q2[:, t, :], 0, t, gcol[:, 1:2]) for t in range(KT)]
                       + [(k2[:, t, :], k2[:, t, :], 1, t, gains[:, G_DK:G_DK + 1]) for t in range(KT)], sel=0, sizes=[8, 8]),
            "kx": dict(tiles=[(kw, ki, 0, 0, None)], sel=0, sizes=[1]),
            "sq": dict(tiles=[(q2[:, t, :], q2[:, t, :], 0, t, gcol[:, 2:3]) for t in range(KT)]
                       + [(k2[:, t, :], k2[:, t, :], 1, t, gains[:, G_SK:G_SK + 1]) for t in range(KT)], sel=0, sizes=[8, 8]),
            "gla": dict(tiles=[(gla_o[:, t, :], 4 + t, 0, t, gains[:, G_GLA:G_GLA + 1]) for t in range(4)], sel=1, sizes=[4]),
            "sub": dict(tiles=[(q2[:, t, :], t, 0, t, gcol[:, 3:4]) for t in range(KT)], sel=1, sizes=[8]),
            "cq": dict(tiles=[(cq[:, t, :], t, 0, t, gains[:, G_CQ + t:G_CQ + t + 1]) for t in range(2)], sel=2, sizes=[2]),
        }

        def ngain(p, t):
            g = NORM_GAIN[p] + t
            return gains[:, g:g + 1]

        @block.tensor
        def _(pe):
            def mm(out, lhsT, rhs, start=True, stop=True):
                return pe.matmul(out, lhsT, rhs, start=start, stop=stop)

            def mm3(out, w, a, first, last):
                mm(out, w[0], a[0], first, False)
                mm(out, w[0], a[1], False, False)
                return mm(out, w[1], a[0], False, last)

            def begin(c, j=0):
                wait_lo(pe, c, j)
                if c >= 2 or not isinstance(j, int):
                    pe.wait_ge(sem("evac"), 2 * j + (c - 1))

            def wtile(c, k, m, width=P):
                at0 = k * BC + m * P
                return w_hi[:, c % 2, at0:at0 + width], w_lo[:, c % 2, at0:at0 + width]

            def blk(c, j=0, a=(xg_hi, xg_lo), nk=KT, ms=(0, 1), waits={}):
                begin(c, j)
                for k in range(nk):
                    for s_, v in waits.get(k, ()):
                        pe.wait_ge(s_, v)
                    for m in ms:
                        last = mm3(two(c, m), wtile(c, k, m), (a[0][:, k, :], a[1][:, k, :]), k == 0, k == nk - 1)
                last.then_inc(sem("pe_blk"), 1)

            def tok_part(c, m, width, per_bank):
                for t in range(NT):
                    dst = two(c, m + t // per_bank)[:, (t % per_bank) * width:(t % per_bank + 1) * width]
                    ts = slice(t * P, (t + 1) * P)
                    for k in range(KT):
                        last = mm3(dst, (xg_hi[:, k, ts], xg_lo[:, k, ts]), wtile(c, k, m, width), k == 0, k == KT - 1)
                return last

            def tok_blk(c):
                begin(c)
                tok_part(c, 0, BC, 2).then_inc(sem("pe_blk"), 1)

            def xg_waits(p):
                return {k: [(sem("xg_done"), 8 * p + k + 1)] for k in range(KT)}

            def stats(p):
                pe.wait_ge(sem("ssq_done"), 7 * (p + 1))
                last = mm(bank[4], mean[:], ssq[:])
                if p in (1, 4, 6):
                    for t in range(NT):
                        last = mm(bank[5][:, t:t + 1], ssq[:, t * P:(t + 1) * P], mean[:, 0:1])
                last.then_inc(sem("ms"), 1)

            hcount = [0]

            def ffn(name, groups, p, gated, between=None):
                for g, tiles in enumerate(groups):
                    c, nb = at[name, g, "up"], tiles if gated else tiles // 2
                    if g == 0:
                        blk(c, waits=xg_waits(p))
                        stats(p)
                        blk(c + 1)
                    with pe.Fori(1 if g == 0 else 0, nb // 2) as j:
                        blk(c, j)
                        blk(c + 1, j)
                    h0 = hcount[0]
                    hcount[0] += tiles // 2
                    waits = {0: [(sem("h_done"), h0 + tiles // 2 - 1)], tiles - 2: [(sem("h_done"), h0 + tiles // 2)]}
                    c = at[name, g, "down"]
                    with pe.Fori(0, 2) as j:
                        for s in range(2):
                            blk(c + s, j, (h_hi, h_lo), tiles, waits=waits)
                    if between and g == 0:
                        between()

            def gn_stats(name):
                d = GN[name]
                for i, (z, o, grp, idx, g) in enumerate(d["tiles"]):
                    pe.wait_ge(*use(name, "_sq", i + 1))
                    mm(bank[4 + grp][0:16, :], sel[:, d["sel"] * KT + idx, :], sq[:, i % 2, :], idx == 0,
                       idx == d["sizes"][grp] - 1).then_inc(use(name, "_msq")[0], 1)

            def gn_apply(name, rope):
                tiles = GN[name]["tiles"]

                def rotate(i):
                    pe.wait_ge(*use(name, "_nrm", i + 1))
                    if i >= 2:
                        pe.wait_ge(*use(name, "_sin", i - 1))
                    mm(bank[4 + i % 2], rot[:, rope, :], buf_a[:, i % 2, :]).then_inc(use(name, "_rot")[0], 1)

                pe.wait_ge(*use(name, "_rs", 1))
                for i, (z, o, grp, idx, g) in enumerate(tiles):
                    if i >= 2:
                        pe.wait_ge(*use(name, "_nrm", i - 1))
                    mm(bank[6 + i % 2], spread[:, idx * P:(idx + 1) * P], rs16[grp]).then_inc(use(name, "_bc")[0], 1)
                    if rope is not None and i >= 1:
                        rotate(i - 1)
                if rope is not None:
                    rotate(len(tiles) - 1)

            pe.wait_ge(sem("const_a"), 16)
            pe.wait_ge(sem("gain_rows"), 16 * 30)
            pe.transpose(bank[7][:, 0:G_ROWS], buf_d[0:G_ROWS, 0, 0:P], ident[0:G_ROWS, 0:G_ROWS]).then_inc(sem("gains_t"), 1)
            pe.wait_ge(sem("x_in"), 16 * NT)
            for k in range(KT):
                if k >= 3:
                    pe.wait_ge(sem("x_copied"), k - 2)
                for n in range(NT):
                    last = pe.transpose(bank[4 + k % 3][:, n * P:(n + 1) * P],
                                        arena[:, n * D + k * P:n * D + (k + 1) * P], ident[:])
                last.then_inc(sem("x_tr"), 1)

            def setup():
                pe.wait_ge(sem("const_c"), 48)
                mm(bank[7], mean[0:1, :], arena[0:1, 1024:1536]).then_inc(sem("pos_mm"), 1)
                pe.wait_ge(sem("lam_prod"), 1)
                mm(bank[6][:, 0:1], arena[:, 2048:2176], sm[:, 64:65])
                mm(bank[6][:, 1:2], arena[:, 2176:2304], sm[:, 64:65])
                mm(bank[6][:, 8:16], mean[0:8, :], sm[0:8, 66:74]).then_inc(sem("lam_mm"), 1)

            ffn("ffn1", GROUPS1, 0, True, between=setup)

            c = at["mix"]
            blk(c, waits=xg_waits(1))
            stats(1)
            blk(c + 1)
            begin(c + 2)
            for k in range(KT):
                mm3(two(c + 2, 0), wtile(c + 2, k, 0), (xg_hi[:, k, :], xg_lo[:, k, :]), k == 0, k == KT - 1)
            tok_part(c + 2, 1, P, 4).then_inc(sem("pe_blk"), 1)
            blk(c + 3)
            blk(c + 4)
            tok_blk(c + 5)
            tok_blk(c + 6)
            blk(c + 7, ms=(0,))
            blk(c + 8)
            blk(c + 9)
            pe.wait_ge(sem("evac"), c + 8)
            pe.wait_ge(sem("mix_const"), 32)
            for m in range(2):
                mm(bank[6 + m], wgu[:, m * P:(m + 1) * P], glr).then_inc(sem("gate_mm"), 1)
            gn_stats("gq")
            pe.wait_ge(sem("gate_read"), 1)
            gn_apply("gq", 0)

            pe.wait_ge(sem("evac"), c + 10)
            pe.wait_ge(*use("gq", "_out", 5))
            pe.wait_ge(sem("kswap"), 32)

            def a1_scores(h):
                half, kv = h % 2, h // 4
                hs = slice(HD * half, HD * half + HD)
                keys = ak if half == kv else ak_swap
                if h >= 2:
                    pe.wait_ge(sem("a1_exp"), h - 1)
                for n in range(NT):
                    dst = bank[2 * (h % 2) + n // 2][:, (n % 2) * 256:(n % 2 + 1) * 256]
                    mm(dst, ident_bf[:], first_mask if n == 0 else band_mask, True, False)
                    q = aq[hs, h // 2, n * P:(n + 1) * P]
                    if n == 0:
                        last = mm(dst[:, P:], q, keys[hs, 0:P], False, True)
                    else:
                        last = mm(dst, q, keys[hs, (n - 1) * P:(n + 1) * P], False, True)
                last.then_inc(sem("a1_s"), 1)

            def a1_pt(h):
                return free_x[:, 4 + 2 * (h % 2):6 + 2 * (h % 2), :].rearrange("p a (b q) -> p (a b) q", q=P)

            def a1_p(h):
                return free_x[:, 2 * (h % 2):2 * (h % 2) + 2, :].rearrange("p a (b q) -> p (a b) q", q=P)

            def a1_transpose(h):
                pe.wait_ge(sem("a1_prob"), h + 1)
                if h >= 1:
                    pe.wait_ge(sem("a1_ptc"), h)
                for i in range(2 * NT):
                    last = pe.transpose(bank[4 + i // 4][:, (i % 4) * P:(i % 4 + 1) * P], a1_p(h)[:, i, :], ident[:])
                last.then_inc(sem("a1_t"), 1)

            def a1_values(h):
                t, hs, kv = h // 2, slice(HD * (h % 2), HD * (h % 2) + HD), h // 4
                pe.wait_ge(sem("a1_ptc"), h + 1)
                if t >= 2:
                    pe.wait_ge(sem("a1_out"), t - 1)
                for n in range(NT):
                    for w in ((1,) if n == 0 else (0, 1)):
                        last = mm(bank[6 + t % 2][hs, n * P:(n + 1) * P], av[:, n - 1 + w, kv * HD:(kv + 1) * HD],
                                  a1_pt(h)[:, 2 * n + w, :], w == 0 or n == 0, w == 1)
                last.then_inc(sem("a1_pv"), 1)

            a1_scores(0)
            for h in range(8):
                if h < 7:
                    a1_scores(h + 1)
                a1_transpose(h)
                if h >= 1:
                    a1_values(h - 1)
            a1_values(7)

            def gla_pairs(base_bank, kmat, qmat, dq, name):
                for h in range(4):
                    hs = slice(HD * (h % 2), HD * (h % 2) + HD)
                    for J in range(NT - dq):
                        last = mm(bank[base_bank + h][:, J * P:(J + 1) * P],
                                  kmat[hs, h // 2, J * P:(J + 1) * P], qmat[hs, h // 2, (J + dq) * P:(J + dq + 1) * P])
                last.then_inc(sem(name), 1)

            pe.wait_ge(sem("a1_out"), 4)
            for i in range(len(LEVELS)):
                pe.wait_ge(sem("gla_k"), i + 1)
                pe.wait_ge(sem("gla_q"), i + 1)
                if i >= 2:
                    pe.wait_ge(sem("gla_acc"), i - 1)
                gla_pairs(4 * (i % 2), kl[i % 2], ql[i % 2], 0, "gla_s")
            i = len(LEVELS)
            pe.wait_ge(sem("gla_acc"), i - 1)
            gla_pairs(4 * (i % 2), gk, gq, 0, "gla_s")
            pe.wait_ge(sem("gla_kx"), 1)
            pe.wait_ge(sem("gla_q"), len(LEVELS) + 1)
            pe.wait_ge(sem("gla_acc"), len(LEVELS))
            gla_pairs(0, gkx, ql[0], 1, "gla_x")
            pe.wait_ge(sem("gla_acc"), len(LEVELS) + 1)
            pe.wait_ge(sem("gla_q"), len(LEVELS) + 2)
            gla_pairs(4, gkx, ql[1], 2, "gla_x")
            pe.wait_ge(sem("gla_q"), len(LEVELS) + 3)
            pe.wait_ge(sem("gla_xc"), 1)
            gla_pairs(0, gkx, dl[0], 3, "gla_x")
            pe.wait_ge(sem("gla_xc"), 3)
            xoff = {1: 0, 2: 12, 3: 20}
            for h in range(4):
                for I in range(NT):
                    for J in range(I + 1):
                        a = acc_at[:, h, I, :] if I == J else cross_at[:, xoff[I - J] + h * (NT - I + J) + J, :]
                        last = mm(bank[h][:, I * P:(I + 1) * P], gv[:, J, h * P:(h + 1) * P], a, J == 0, J == I)
                last.then_inc(sem("gla_pv"), 1)
            gn_stats("gla")
            gn_apply("gla", None)

            def wout(name, waits):
                for i in range(4):
                    blk(at[name] + i, a=(h_hi, h_lo), waits=waits if i == 0 else {})

            wout("wout1", {4 + i: [use("gla", "_out", i + 1)] for i in range(4)})
            ffn("ffn2", GROUPS1, 2, True)

            pe.wait_ge(sem("p_in"), 32)
            for k in range(2):
                for n in range(NT):
                    last = pe.transpose(bank[6 + k][:, n * P:(n + 1) * P], arena[:, n * 256 + k * P:n * 256 + (k + 1) * P], ident[:])
                last.then_inc(sem("p_tr"), 1)
            pe.wait_ge(sem("p_lo"), 1)
            for i in range(4):
                blk(at["proj"] + i, a=(h_hi, h_lo), nk=2)
            blk(at["gate"], waits=xg_waits(3))
            stats(3)
            for i in range(1, 4):
                blk(at["gate"] + i)
            pe.wait_ge(sem("emb_ssq"), 7)
            mm(bank[5], mean[:], buf_c[:, 0, :]).then_inc(sem("emb_ms"), 1)
            pe.wait_ge(sem("pos_f32"), 1)
            mm(bank[7], mean[0:1, :], buf_b[0:1, 1, :]).then_inc(sem("pos_mm"), 1)

            c = at["diff"]
            blk(c, waits=xg_waits(4))
            stats(4)
            for i in range(1, 8):
                blk(c + i)
            for i in range(8, 12):
                tok_blk(c + i)
            gn_stats("dq")
            gn_apply("dq", 1)

            def pairs_attention(name, dsa):
                units = [(g, n) for g in range(KT) for n in range(NT)]

                def scores(u):
                    g, n = units[u]
                    w = (n + 1) * P
                    if u >= 2:
                        pe.wait_ge(*use(name, "_exp", u - 1))
                    for cc in range(2):
                        hs = slice(HD * cc, HD * cc + HD)
                        dst = bank[2 * (u % 2) + cc]
                        mm(dst[:, 0:w], q2[hs, g, n * P:(n + 1) * P], k2[hs, g, 0:w], True, False)
                        if dsa and n:
                            last = mm(dst[:, 0:w], ident_bf[:], kmask[:, n - 1, 0:w], False, True)
                        else:
                            last = mm(dst[:, n * P:w], ident_bf[:], chunk_mask, False, True)
                    last.then_inc(use(name, "_s")[0], 1)

                def transposes(u):
                    g, n = units[u]
                    pe.wait_ge(*use(name, "_prob", u + 1))
                    if dsa:
                        if u >= 1:
                            pe.wait_ge(*use(name, "_ptc", u))
                        for cc in range(2):
                            for J in range(n + 1):
                                last = pe.transpose(bank[4 + cc][:, J * P:(J + 1) * P],
                                                    free_x[:, 2 * (u % 2) + cc, J * P:(J + 1) * P], ident[:])
                    else:
                        if u >= 2:
                            pe.wait_ge(*use(name, "_ptc", u - 1))
                        for J in range(n + 1):
                            last = pe.transpose(bank[4 + u % 2][:, J * P:(J + 1) * P],
                                                free_x[:, 4 + u % 2, J * P:(J + 1) * P], ident[:])
                    last.then_inc(use(name, "_t")[0], 1)

                def values(u):
                    g, n = units[u]
                    pe.wait_ge(*use(name, "_ptc", u + 1))
                    if n == 0 and g >= 2:
                        pe.wait_ge(*use(name, "_oc", g - 1))
                    for cc in range(2 if dsa else 1):
                        for J in range(n + 1):
                            if dsa:
                                dst = bank[6 + g % 2][HD * cc:HD * cc + HD, n * P:(n + 1) * P]
                                v = v2[:, J, (2 * g + cc) * HD:(2 * g + cc + 1) * HD]
                            else:
                                dst, v = bank[6 + g % 2][:, n * P:(n + 1) * P], v2[:, J, g * P:(g + 1) * P]
                            last = mm(dst, v, free_x[:, 8 + 2 * (u % 2) + cc, J * P:(J + 1) * P], J == 0, J == n)
                    last.then_inc(use(name, "_pv")[0], 1)

                scores(0)
                for u in range(len(units)):
                    if u + 1 < len(units):
                        scores(u + 1)
                    transposes(u)
                    if u >= 1:
                        values(u - 1)
                values(len(units) - 1)

            pe.wait_ge(sem("evac"), c + 12)
            pe.wait_ge(*use("dq", "_out", 16))
            pairs_attention("a2", False)
            gn_stats("sub")
            gn_apply("sub", None)
            wout("wout2", {k: [use("sub", "_out", k + 1)] for k in range(KT)})
            ffn("mlp0", GROUPS2, 5, False)

            c = at["dsa"]
            blk(c, waits=xg_waits(6))
            stats(6)
            blk(c + 1, ms=(0,))
            for i in range(2, 6):
                blk(c + i)
            for i in range(6, 10):
                tok_blk(c + i)
            pe.wait_ge(sem("evac"), c + 2)
            for n in range(NT):
                last = pe.transpose(bank[6][:, n * P:(n + 1) * P], kw[:, n * P:(n + 1) * P], ident[:])
            last.then_inc(sem("widx_t"), 1)
            gn_stats("cq")
            pe.wait_ge(sem("widx_read"), 1)
            gn_apply("cq", None)
            for i in range(6):
                blk(at["uq"] + i, a=(cq_hi, cq_lo), nk=2, waits={0: [use("cq", "_out", 2)]} if i == 0 else {})
            gn_stats("kx")
            gn_apply("kx", 1)
            for i in range(4):
                if i >= 2:
                    pe.wait_ge(*use("qi", "_sin", i - 1))
                else:
                    pe.wait_ge(*use("kx", "_out", 1))
                    pe.wait_ge(sem("evac"), at["uq"] + 6)
                mm(bank[4 + i % 2], rot[:, 1, :], qi[:, i, :]).then_inc(use("qi", "_rot")[0], 1)
            pe.wait_ge(*use("qi", "_out", 4))
            pe.wait_ge(sem("kswap"), 48)
            u = 0
            for n in range(1, NT):
                for hh in range(8):
                    if u >= 2:
                        pe.wait_ge(sem("dot_relu"), u - 1)
                    hs = slice(HD * (hh % 2), HD * (hh % 2) + HD)
                    mm(bank[6 + u % 2][:, 0:(n + 1) * P], qi[hs, hh // 2, n * P:(n + 1) * P],
                       ki[hs, 0:(n + 1) * P]).then_inc(sem("dots"), 1)
                    u += 1
            gn_stats("sq")
            pe.wait_ge(sem("dot_relu"), 24)
            gn_apply("sq", 1)
            pe.wait_ge(*use("sq", "_out", 16))
            pe.wait_ge(sem("kmask_done"), 3)
            pairs_attention("a3", True)
            wout("wout3", {k: [use("a3", "_oc", k + 1)] for k in range(KT)})
            ffn("mlp1", GROUPS2, 7, False)
            pe.wait_ge(sem("evac"), NB)
            for n in range(NT):
                for b in range(2):
                    u = 2 * n + b
                    if u >= 4:
                        pe.wait_ge(sem("y_copied"), u - 3)
                    for k in range(4):
                        last = pe.transpose(bank[4 + u % 4][:, k * P:(k + 1) * P], x_res[:, 4 * b + k, n * P:(n + 1) * P], ident[:])
                    last.then_inc(sem("y_tr"), 1)

        @block.scalar
        def _(act):
            def a(out_, in_, f, **kw):
                return act.activation(out_, in_, f, **kw)

            def fin(p, t):
                a(xg_hi[:, t, :], x_res[:, t, :], ACT.Copy, scale=ngain(p, t)).then_inc(sem("xg_hi_done"), 1)
                if t >= 2:
                    act.wait_ge(sem("ssq_done"), 7 * p + max(1, t - 2))
                a(sq[:, t % 2, :], x_res[:, t, :], ACT.Square).then_inc(sem("sq_done"), 1)

            def stats(p):
                act.wait_ge(sem("ms"), p + 1)
                last = a(rstd[:], bank[4], ACT.Sqrt, bias=eps[:])
                if p in (1, 4, 6):
                    last = a(rstd_tok[:], bank[5][:, 0:NT], ACT.Sqrt, bias=eps[:])
                last.then_inc(sem("rms"), 1)

            hcount, scount = [0], [0]

            def ffn(name, groups, p, gated, p_next, between=None):
                stats(p)
                for g, tiles in enumerate(groups):
                    c, h0, s0 = at[name, g, "up"], hcount[0], scount[0]
                    hcount[0] += tiles // 2
                    if gated:
                        scount[0] += tiles // 2
                        with act.Fori(0, tiles // 2) as j:
                            act.wait_ge(sem("evac"), 2 * j + (c + 1))
                            a(buf_c[:], buf_a[:], ACT.Silu).then_inc(sem("silu"), 1)
                            hi(act, c + 2, j)
                            act.wait_ge(sem("hmul"), j + (h0 + 1))
                            a(h_hi[:, bass.ds(2 * j, 2), :], buf_d[:], ACT.Copy).then_inc(sem("h_hi_done"), 1)
                            hi(act, c + 3, j)
                    else:
                        with act.Fori(0, tiles // 4) as j:
                            for s_ in range(2):
                                act.wait_ge(sem("hmul"), 2 * j + (h0 + s_ + 1))
                                a(h_hi[:, bass.ds(4 * j + 2 * s_, 2), :], buf_d[:], ACT.Copy).then_inc(sem("h_hi_done"), 1)
                                hi(act, c + 2 + s_, j)
                    c = at[name, g, "down"]
                    for i in range(4):
                        if g == len(groups) - 1 and p_next is not None:
                            act.wait_ge(sem("evac"), c + i + 1)
                            fin(p_next, 2 * i)
                            fin(p_next, 2 * i + 1)
                        hi(act, c + 2 + i)
                    if between and g == 0:
                        between()

            def gn_stats(name):
                d = GN[name]
                for i, (z, o, grp, idx, g) in enumerate(d["tiles"]):
                    if i >= 2:
                        act.wait_ge(*use(name, "_msq", i - 1))
                    a(sq[:, i % 2, :], z, ACT.Square).then_inc(use(name, "_sq")[0], 1)
                act.wait_ge(*use(name, "_msq", len(d["tiles"])))
                for grp in range(len(d["sizes"])):
                    last = a(rs16[grp], bank[4 + grp][0:16, :], ACT.Sqrt, bias=eps[0:16, :])
                last.then_inc(use(name, "_rms")[0], 1)

            def gn_split(name, dst, src, ready):
                for i, (z, o, grp, idx, g) in enumerate(GN[name]["tiles"]):
                    act.wait_ge(*use(name, ready, i + 1))
                    a(dst[:, o, :], src[:, i % 2, :], ACT.Copy).then_inc(use(name, "_hi")[0], 1)

            def tables(k):
                act.wait_ge(sem("angles"), k + 1)
                a(sin_t[:], sin_t[:], ACT.Sin)
                a(cos_t[:], cos_t[:], ACT.Sin).then_inc(sem("tables"), 1)

            def setup():
                act.wait_ge(sem("lam_mm"), 1)
                a(sm[:, 74:76], bank[6][:, 0:2], ACT.Exp).then_inc(sem("lam_exp"), 1)
                tables(0)

            act.wait_ge(sem("memsets"), 1)
            hi(act, 0)
            act.wait_ge(sem("gains_c"), 1)
            for t in range(KT):
                act.wait_ge(sem("x_copied"), t + 1)
                fin(0, t)
            hi(act, 1)
            ffn("ffn1", GROUPS1, 0, True, 1, between=setup)

            c = at["mix"]
            stats(1)
            for i in range(10):
                hi(act, c + 2 + i)
            act.wait_ge(sem("evac"), c + 10)
            for m in range(2):
                a(gog[:, 2 * m:2 * m + 2, :], gog[:, 2 * m:2 * m + 2, :], ACT.Silu).then_inc(sem("gog_silu"), 1)
            act.wait_ge(sem("gate_abs"), 1)
            a(buf_c[:], buf_c[:], ACT.Exp, scale=-1.0).then_inc(sem("gate_exp"), 1)
            act.wait_ge(sem("gate_exp"), 1)
            a(buf_c[:], buf_c[:], ACT.Ln, bias=one[:]).then_inc(sem("gate_ln"), 1)
            gn_stats("gq")

            def a1_exp(h):
                so = 16 * (h % 2)
                act.wait_ge(sem("a1_m"), h + 1)
                if h >= 2:
                    act.wait_ge(sem("a1_t"), h - 1)
                for n in range(NT):
                    a(free_x[:, 2 * (h % 2) + n // 2, (n % 2) * 256:(n % 2 + 1) * 256],
                      bank[2 * (h % 2) + n // 2][:, (n % 2) * 256:(n % 2 + 1) * 256], ACT.Exp,
                      bias=sm[:, so + 4 + n:so + 5 + n], accum_out=sm[:, so + 8 + n:so + 9 + n])
                a(sm[:, so + 12:so + 16], sm[:, so + 4:so + 8], ACT.Exp,
                  bias=sinks[:, h:h + 1]).then_inc(sem("a1_exp"), 1)

            def a1_ptc(h):
                act.wait_ge(sem("a1_t"), h + 1)
                if h >= 2:
                    act.wait_ge(sem("a1_pv"), h - 1)
                a(free_x[:, 4 + 2 * (h % 2):6 + 2 * (h % 2), :], psum[:, 4:6, :], ACT.Copy).then_inc(sem("a1_ptc"), 1)

            def a1_hi(t):
                act.wait_ge(sem("a1_pv"), 2 * t + 2)
                a(h_hi[:, t, :], bank[6 + t % 2], ACT.Copy).then_inc(sem("a1_hi"), 1)

            a1_exp(0)
            for h in range(8):
                if h < 7:
                    a1_exp(h + 1)
                a1_ptc(h)
                if h % 2 == 0 and h >= 2:
                    a1_hi(h // 2 - 1)
            a1_hi(3)

            for i in range(len(LEVELS)):
                act.wait_ge(sem("gla_d"), i + 1)
                a(dl[i % 2], dl[i % 2], ACT.Exp, scale=1 / 16).then_inc(sem("gla_e"), 1)
            act.wait_ge(sem("gla_d"), 8)
            a(dl[1], dl[1], ACT.Exp, scale=1 / 16).then_inc(sem("gla_e"), 1)
            act.wait_ge(sem("gla_q"), 7)
            act.wait_ge(sem("gla_k"), 7)
            a(dl[0], cum.rearrange("p (m t) -> p m t", t=S), ACT.Exp, scale=1 / 16).then_inc(sem("gla_e"), 1)
            act.wait_ge(sem("gla_d"), 9)
            a(dl[1][:, :, 256:512], dl[1][:, :, 256:512], ACT.Exp, scale=1 / 16).then_inc(sem("gla_e"), 1)
            act.wait_ge(sem("gla_d"), 10)
            a(dl[0][:, :, 384:512], dl[0][:, :, 384:512], ACT.Exp, scale=1 / 16).then_inc(sem("gla_e"), 1)
            at0 = 0
            for dq in (1, 2, 3):
                w = NT - dq
                act.wait_ge(sem("gla_x"), dq)
                bk = 4 * ((dq - 1) % 2)
                a(cross_at[:, at0:at0 + 4 * w, :].rearrange("p (h j) i -> p h (j i)", h=4),
                  psum[:, bk:bk + 4, 0:w * P], ACT.Copy).then_inc(sem("gla_xc"), 1)
                at0 += 4 * w
            act.wait_ge(sem("gla_oc"), 4)
            gn_stats("gla")
            gn_split("gla", h_hi, buf_b, "_pre")

            def wout(name, p):
                c = at[name]
                for i in range(4):
                    act.wait_ge(sem("evac"), c + i + 1)
                    fin(p, 2 * i)
                    fin(p, 2 * i + 1)
                    hi(act, c + 2 + i)

            wout("wout1", 2)
            ffn("ffn2", GROUPS1, 2, True, 3)

            act.wait_ge(sem("p_tr"), 2)
            a(h_hi[:, 0:2, :], psum[:, 6:8, :], ACT.Copy).then_inc(sem("p_hi"), 1)
            c = at["proj"]
            act.wait_ge(sem("ssq_done"), 28)
            for i in range(4):
                act.wait_ge(sem("evac"), c + i + 1)
                for t in (2 * i, 2 * i + 1):
                    if t >= 2:
                        act.wait_ge(sem("emb_ssq"), max(1, t - 2))
                    a(sq[:, t % 2, :], emb[:, t, :], ACT.Square).then_inc(sem("emb_sq"), 1)
                hi(act, c + 2 + i)
            stats(3)
            c = at["gate"]
            for i in range(4):
                act.wait_ge(sem("evac"), c + i + 1)
                a(sig[:, 2 * i:2 * i + 2, :], buf_a[:], ACT.Sigmoid).then_inc(sem("sig"), 1)
                hi(act, c + 2 + i)
            act.wait_ge(sem("emb_ms"), 1)
            a(buf_c[:, 1, :], bank[5], ACT.Sqrt, bias=eps[:]).then_inc(sem("emb_rms"), 1)
            tables(1)
            for t in range(KT):
                act.wait_ge(sem("ple_x"), t + 1)
                fin(4, t)

            c = at["diff"]
            stats(4)
            for i in range(12):
                hi(act, c + 2 + i)
            act.wait_ge(sem("evac"), c + 8)
            gn_stats("dq")

            def pairs_attention(name, dsa):
                units = [(g, n) for g in range(KT) for n in range(NT)]

                def exp(u):
                    w, so = (units[u][1] + 1) * P, 16 * (u % 2)
                    act.wait_ge(*use(name, "_m", u + 1))
                    if u >= 2:
                        act.wait_ge(*use(name, "_t", u - 1))
                    for cc in range(2):
                        last = a(free_x[:, 2 * (u % 2) + cc, 0:w], bank[2 * (u % 2) + cc][:, 0:w], ACT.Exp,
                                 bias=sm[:, so + cc:so + cc + 1], accum_out=sm[:, so + 2 + cc:so + 3 + cc])
                    last.then_inc(use(name, "_exp")[0], 1)

                def ptc(u):
                    w = (units[u][1] + 1) * P
                    act.wait_ge(*use(name, "_t", u + 1))
                    if u >= 2:
                        act.wait_ge(*use(name, "_pv", u - 1))
                    if dsa:
                        last = a(free_x[:, 8 + 2 * (u % 2):10 + 2 * (u % 2), 0:w], psum[:, 4:6, 0:w], ACT.Copy)
                    else:
                        last = a(free_x[:, 8 + 2 * (u % 2), 0:w], bank[4 + u % 2][:, 0:w], ACT.Copy)
                    last.then_inc(use(name, "_ptc")[0], 1)

                def out_tile(g):
                    act.wait_ge(*use(name, "_pv", 4 * (g + 1)))
                    if dsa:
                        a(h_hi[:, g, :], bank[6 + g % 2], ACT.Copy).then_inc(use(name, "_hi")[0], 1)
                    else:
                        a(q2[:, g, :], bank[6 + g % 2], ACT.Copy).then_inc(use(name, "_oc")[0], 1)

                exp(0)
                for u, (g, n) in enumerate(units):
                    if u + 1 < len(units):
                        exp(u + 1)
                    ptc(u)
                    if n == 1 and g >= 1:
                        out_tile(g - 1)
                out_tile(KT - 1)

            pairs_attention("a2", False)
            act.wait_ge(*use("a2", "_oc", 8))
            gn_stats("sub")
            gn_split("sub", h_hi, buf_a, "_nrm")
            wout("wout2", 5)
            ffn("mlp0", GROUPS2, 5, False, 6)

            c = at["dsa"]
            stats(6)
            for i in range(10):
                hi(act, c + 2 + i)
            act.wait_ge(sem("evac"), c + 1)
            gn_stats("cq")
            gn_split("cq", cq_hi, buf_a, "_nrm")
            for i in range(6):
                hi(act, at["uq"] + 2 + i)
            gn_stats("kx")
            u = 0
            for n in range(1, NT):
                for hh in range(8):
                    w = (n + 1) * P
                    act.wait_ge(sem("dots"), u + 1)
                    if u >= 2:
                        act.wait_ge(sem("dot_acc"), u - 1)
                    a(buf_c[:, u % 2, 0:w], bank[6 + u % 2][:, 0:w], ACT.Relu).then_inc(sem("dot_relu"), 1)
                    u += 1
            gn_stats("sq")
            pairs_attention("a3", True)
            wout("wout3", 7)
            ffn("mlp1", GROUPS2, 7, False, None)
            for u in range(1, 2 * NT, 2):
                act.wait_ge(sem("y_tr"), u + 1)
                n, b = u // 2, u % 2
                act.wait_ge(sem("y_copied"), u)
                a(arena[:, n * D + b * S:n * D + b * S + S], bank[4 + u % 4], ACT.Copy).then_inc(sem("y_copied"), 1)

        @block.vector
        def _(dve):
            chain = [0]

            def link(ins):
                chain[0] += 1
                ins.then_inc(sem("dve_chain"), 1)
                dve.wait_ge(sem("dve_chain"), chain[0])

            def tt(o, x, y, op):
                return dve.tensor_tensor(o, x, y, op)

            def stt(o, x, s_, y, op0, op1):
                return dve.scalar_tensor_tensor(out=o, in0=x, scalar=s_, in1=y, op0=op0, op1=op1)

            def ts(o, x, s1, s2, op0, op1=None):
                if op1 is None:
                    return dve.tensor_scalar(o, x, s1, None, op0)
                return dve.tensor_scalar(o, x, s1, s2, op0, op1)

            def fin(p, t):
                dve.wait_ge(sem("xg_hi_done"), 8 * p + t + 1)
                stt(xg_lo[:, t, :], x_res[:, t, :], ngain(p, t), xg_hi[:, t, :].bitcast(F32),
                    ALU.mult, ALU.subtract).then_inc(sem("xg_done"), 1)

            def stats(p):
                dve.wait_ge(sem("rms"), p + 1)
                link(dve.reciprocal(rstd[:], rstd[:]))
                if p in (1, 4, 6):
                    link(dve.reciprocal(rstd_tok[:], rstd_tok[:]))

            def evac_scaled(c, dst, j=0, ms=(0, 1)):
                dve.wait_ge(sem("pe_blk"), 2 * j + (c + 1))
                for m in ms:
                    last = tt(dst[:, m, :], two(c, m), rstd[:], ALU.mult)
                last.then_inc(sem("evac"), 1)

            def evac_tok(c, dst, f0):
                dve.wait_ge(sem("pe_blk"), c + 1)
                for t in range(NT):
                    last = ts(dst[:, t, f0:f0 + BC], two(c, t // 2)[:, (t % 2) * BC:(t % 2 + 1) * BC],
                              rstd_tok[:, t:t + 1], None, ALU.mult)
                last.then_inc(sem("evac"), 1)

            def residual(c, i, scale, p_next):
                dve.wait_ge(sem("pe_blk"), c + i + 1)
                for m in range(2):
                    t = 2 * i + m
                    last = stt(x_res[:, t, :], two(c + i, m), scale, x_res[:, t, :], ALU.mult, ALU.add)
                last.then_inc(sem("evac"), 1)
                if p_next is not None:
                    fin(p_next, 2 * i)
                    fin(p_next, 2 * i + 1)
                lo(dve, c + 2 + i)

            hcount, scount = [0], [0]

            def ffn(name, groups, p, gated, scale, p_next, between=None):
                stats(p)
                for g, tiles in enumerate(groups):
                    c, h0, s0 = at[name, g, "up"], hcount[0], scount[0]
                    hcount[0] += tiles // 2
                    if gated:
                        scount[0] += tiles // 2
                        with dve.Fori(0, tiles // 2) as j:
                            evac_scaled(c, buf_a, j)
                            lo(dve, c + 2, j)
                            evac_scaled(c + 1, buf_b, j)
                            dve.wait_ge(sem("evac"), 2 * j + (c + 2))
                            dve.wait_ge(sem("silu"), j + (s0 + 1))
                            tt(buf_d[:], buf_b[:], buf_c[:], ALU.mult).then_inc(sem("hmul"), 1)
                            dve.wait_ge(sem("h_hi_done"), j + (h0 + 1))
                            tt(h_lo[:, bass.ds(2 * j, 2), :], buf_d[:], h_hi[:, bass.ds(2 * j, 2), :].bitcast(F32),
                               ALU.subtract).then_inc(sem("h_done"), 1)
                            lo(dve, c + 3, j)
                    else:
                        with dve.Fori(0, tiles // 4) as j:
                            for s_ in range(2):
                                evac_scaled(c + s_, buf_b, j)
                                dve.wait_ge(sem("evac"), 2 * j + (c + s_ + 1))
                                stt(buf_d[:], buf_b[:], 0.0, buf_b[:], ALU.max, ALU.mult).then_inc(sem("hmul"), 1)
                                dve.wait_ge(sem("h_hi_done"), 2 * j + (h0 + s_ + 1))
                                ht = bass.ds(4 * j + 2 * s_, 2)
                                tt(h_lo[:, ht, :], buf_d[:], h_hi[:, ht, :].bitcast(F32),
                                   ALU.subtract).then_inc(sem("h_done"), 1)
                                lo(dve, c + 2 + s_, j)
                    c = at[name, g, "down"]
                    for i in range(4):
                        residual(c, i, scale, p_next if g == len(groups) - 1 else None)
                    if between and g == 0:
                        between()

            def gn_rsqrt(name):
                dve.wait_ge(*use(name, "_rms", 1))
                for grp in range(len(GN[name]["sizes"])):
                    last = dve.reciprocal(rs16[grp], rs16[grp])
                last.then_inc(use(name, "_rs")[0], 1)

            def gn_scale(name, i):
                z, o, grp, idx, g = GN[name]["tiles"][i]
                dve.wait_ge(*use(name, "_bc", i + 1))
                if g is None:
                    ins = tt(buf_a[:, i % 2, :], bank[6 + i % 2], z, ALU.mult)
                else:
                    ins = stt(buf_a[:, i % 2, :], bank[6 + i % 2], g, z, ALU.mult, ALU.mult)
                ins.then_inc(use(name, "_nrm")[0], 1)

            def rope_out(name, i, o):
                dve.wait_ge(*use(name, "_rot", i + 1))
                tt(buf_b[:, i % 2, :], bank[4 + i % 2], sin_t[:], ALU.mult).then_inc(use(name, "_sin")[0], 1)
                dve.wait_ge(*use(name, "_sin", i + 1))
                dve.wait_ge(*use(name, "_cos", i + 1))
                tt(o, buf_b[:, i % 2, :], buf_c[:, i % 2, :], ALU.add).then_inc(use(name, "_out")[0], 1)

            def gn_rope(name):
                gn_rsqrt(name)
                tiles = GN[name]["tiles"]
                for i in range(len(tiles)):
                    gn_scale(name, i)
                    if i:
                        rope_out(name, i - 1, tiles[i - 1][1])
                rope_out(name, len(tiles) - 1, tiles[-1][1])

            def gn_split(name, dhi, dlo, mult=None):
                gn_rsqrt(name)
                for i, (z, o, grp, idx, g) in enumerate(GN[name]["tiles"]):
                    gn_scale(name, i)
                    src = buf_a
                    if mult is not None:
                        dve.wait_ge(*use(name, "_nrm", i + 1))
                        tt(buf_b[:, i % 2, :], buf_a[:, i % 2, :], mult[:, i, :], ALU.mult).then_inc(use(name, "_pre")[0], 1)
                        src = buf_b
                    dve.wait_ge(*use(name, "_hi", i + 1))
                    tt(dlo[:, o, :], src[:, i % 2, :], dhi[:, o, :].bitcast(F32), ALU.subtract).then_inc(use(name, "_out")[0], 1)

            def few_bits(v, bits=8):
                e = math.floor(math.log2(abs(v)))
                q = 2.0 ** (e - bits + 1)
                return math.floor(v / q) * q

            def angles(k):
                dve.wait_ge(sem("pos_mm"), k + 1)
                ang, turns, r = buf_a[:, 0, :], buf_a[:, 1, :], buf_b[:, 0, :]
                link(ts(ang, bank[7], 1024.0, inv[:, k:k + 1], ALU.mult, ALU.mult))
                link(ts(turns, ang, 1 / TWO_PI, ROUND, ALU.mult, ALU.add))
                link(ts(turns, turns, -ROUND, None, ALU.add))
                left, src = TWO_PI, ang
                for _ in range(3):
                    part = few_bits(left)
                    link(stt(r, turns, -part, src, ALU.mult, ALU.add))
                    left, src = left - part, r
                link(stt(r, turns, -left, r, ALU.mult, ALU.add))
                link(ts(sin_t[:], r, 3.1415925, -3.1415925, ALU.min, ALU.max))
                link(stt(cos_t[:], sin_t[:], -1.0, sin_t[:], ALU.mult, ALU.max))
                ts(cos_t[:], cos_t[:], -1.0, math.pi / 2, ALU.mult, ALU.add).then_inc(sem("angles"), 1)

            def setup():
                dve.wait_ge(sem("const_c"), 48)
                dve.wait_ge(sem("const_b"), 16 * 4)
                link(dve.tensor_copy(mask_bf[:], arena[:, 0:5 * P]))
                tt(sm[:, 64:65], gains[:, G_LQ:G_LQ + 1], gains[:, G_LK:G_LK + 1], ALU.mult)
                ts(sm[0:8, 66:74], ident[0:8, 0:8], gains[0:8, G_SINK:G_SINK + 1], None, ALU.mult).then_inc(sem("lam_prod"), 1)
                dve.wait_ge(sem("lam_exp"), 1)
                link(ts(sinks, bank[6][:, 8:16], 1024.0, None, ALU.mult))
                link(tt(gcol[:, 4:5], sm[:, 75:76], sm[:, 74:75], ALU.subtract))
                link(ts(gcol[:, 4:5], gcol[:, 4:5], -LAM_INIT, None, ALU.add))
                angles(0)

            dve.memset(buf_d[:, 0, 0:P], 0.0).then_inc(sem("zeroed"), 1)
            dve.memset(mean[:], 1.0 / D)
            dve.memset(one[:], 1.0)
            dve.memset(eps[:], EPS).then_inc(sem("memsets"), 1)
            dve.wait_ge(sem("memsets"), 1)
            dve.wait_ge(sem("gains_t"), 1)
            dve.tensor_copy(gains[:], bank[7][:, 0:G_ROWS]).then_inc(sem("gains_c"), 1)
            dve.wait_ge(sem("gains_c"), 1)
            for i, g in enumerate((G_QN, G_DQ, G_SQ)):
                ts(gcol[:, i:i + 1], gains[:, g:g + 1], HD ** -0.5, None, ALU.mult)
            ts(gcol[:, 3:4], gains[:, G_SUB:G_SUB + 1], 1.0 - LAM_INIT, None, ALU.mult)
            link(dve.tensor_copy(ident_bf[:], ident[:]))
            for t in range(KT):
                dve.wait_ge(sem("x_tr"), t + 1)
                dve.tensor_copy(x_res[:, t, :], bank[4 + t % 3]).then_inc(sem("x_copied"), 1)
                if t:
                    fin(0, t - 1)
            fin(0, KT - 1)
            lo(dve, 0)
            lo(dve, 1)
            ffn("ffn1", GROUPS1, 0, True, 0.5, 1, between=setup)

            c = at["mix"]
            stats(1)
            for i in range(2):
                evac_scaled(c + i, aq[:, 2 * i:2 * i + 2, :])
                lo(dve, c + 2 + i)
            dve.wait_ge(sem("pe_blk"), c + 3)
            tt(ak, two(c + 2, 0), rstd[:], ALU.mult)
            for t in range(NT):
                last = ts(av[:, t, :], two(c + 2, 1)[:, t * P:(t + 1) * P], rstd_tok[:, t:t + 1], None, ALU.mult)
            last.then_inc(sem("evac"), 1)
            lo(dve, c + 4)
            evac_scaled(c + 3, gq)
            lo(dve, c + 5)
            evac_scaled(c + 4, gk)
            lo(dve, c + 6)
            for i in range(2):
                evac_tok(c + 5 + i, gv, i * BC)
                lo(dve, c + 7 + i)
            dve.wait_ge(sem("pe_blk"), c + 8)
            tt(glr, two(c + 7, 0)[0:16, :], rstd[0:16, :], ALU.mult).then_inc(sem("evac"), 1)
            lo(dve, c + 9)
            for i in range(2):
                evac_scaled(c + 8 + i, gog[:, 2 * i:2 * i + 2, :])
                lo(dve, c + 10 + i)
            dve.wait_ge(sem("gate_mm"), 2)
            for m in range(2):
                last = ts(buf_a[:, m, :], bank[6 + m], gains[:, G_BG + m:G_BG + m + 1], None, ALU.add)
            last.then_inc(sem("gate_read"), 1)
            dve.wait_ge(sem("gate_read"), 1)
            ts(buf_b[:], buf_a[:], 0.0, None, ALU.min)
            stt(buf_c[:], buf_a[:], -1.0, buf_a[:], ALU.mult, ALU.max).then_inc(sem("gate_abs"), 1)
            dve.wait_ge(sem("gate_ln"), 1)
            link(tt(buf_a[:], buf_b[:], buf_c[:], ALU.subtract))
            for m in range(2):
                for t in range(NT):
                    last = dve.tensor_tensor_scan(cum[:, m * S + t * P:m * S + (t + 1) * P], one[:].to_broadcast([P, P]),
                                                  buf_a[:, m, t * P:(t + 1) * P], 0.0, ALU.mult, ALU.add)
            link(last)
            gn_rope("gq")

            def a1_max(h):
                so = 16 * (h % 2)
                dve.wait_ge(sem("a1_s"), h + 1)
                link(dve.tensor_reduce(sm[:, so:so + 4],
                                       psum[:, 2 * (h % 2):2 * (h % 2) + 2, :].rearrange("p a (b k) -> p (a b) k", k=2 * P),
                                       AX.X, ALU.max))
                ts(sm[:, so + 4:so + 8], sm[:, so:so + 4], sinks[:, h:h + 1], -1.0, ALU.max, ALU.mult).then_inc(sem("a1_m"), 1)

            def a1_norm(h):
                so = 16 * (h % 2)
                dve.wait_ge(sem("a1_exp"), h + 1)
                link(tt(sm[:, so + 8:so + 12], sm[:, so + 8:so + 12], sm[:, so + 12:so + 16], ALU.add))
                link(dve.reciprocal(sm[:, so + 8:so + 12], sm[:, so + 8:so + 12]))
                pv = free_x[:, 2 * (h % 2):2 * (h % 2) + 2, :].rearrange("p a (b k) -> p (a b) k", k=2 * P)
                tt(pv, pv, sm[:, so + 8:so + 12].unsqueeze(2).to_broadcast([P, 4, 2 * P]), ALU.mult).then_inc(sem("a1_prob"), 1)

            def a1_lo(t):
                dve.wait_ge(sem("a1_hi"), t + 1)
                tt(h_lo[:, t, :], bank[6 + t % 2], h_hi[:, t, :].bitcast(F32), ALU.subtract).then_inc(sem("a1_out"), 1)

            a1_max(0)
            for h in range(8):
                if h < 7:
                    a1_max(h + 1)
                a1_norm(h)
                if h % 2 == 0 and h >= 2:
                    a1_lo(h // 2 - 1)
            a1_lo(3)

            link(dve.memset(free_x[:, 0:4, :], 0.0))
            dve.wait_ge(sem("mix_const"), 32)
            link(dve.tensor_copy(level[:].rearrange("p a c -> p (a c)"), free_h[:, 12:14, :].rearrange("p a c -> p (a c)")))

            def gla_diff(i):
                s_ = LEVELS[i]
                b = cum.rearrange("p (b w s) -> p b w s", w=2, s=s_)
                d = dl[i % 2].rearrange("p m t -> p (m t)").rearrange("p (b w s) -> p b w s", w=2, s=s_)
                ref = b[:, :, 0, s_ - 1:s_]
                nb_ = 2 * S // (2 * s_)
                if i >= 2:
                    dve.wait_ge(sem("gla_q"), i - 1)
                    dve.wait_ge(sem("gla_k"), i - 1)
                tt(d[:, :, 0, :], ref.to_broadcast([P, nb_, s_]), b[:, :, 0, :], ALU.subtract)
                tt(d[:, :, 1, :], b[:, :, 1, :], ref.to_broadcast([P, nb_, s_]), ALU.subtract).then_inc(sem("gla_d"), 1)

            def gla_keys(i):
                dve.wait_ge(sem("gla_e"), i + 1)
                if i >= 2:
                    dve.wait_ge(sem("gla_s"), i - 1)
                tt(kl[i % 2], gk, dl[i % 2], ALU.mult).then_inc(sem("gla_k"), 1)

            def gla_acc(i):
                dve.wait_ge(sem("gla_s"), i + 1)
                dve.copy_predicated(free_x[:, 0:4, :].rearrange("p a (b q) -> p (a b) q", q=P),
                                    level[:, i:i + 1, :].to_broadcast([P, 16, P]),
                                    psum[:, 4 * (i % 2):4 * (i % 2) + 4, :].rearrange("p a (b q) -> p (a b) q", q=P)
                                    ).then_inc(sem("gla_acc"), 1)

            gla_diff(0)
            nl = len(LEVELS)
            for i in range(nl):
                if i + 1 < nl:
                    gla_diff(i + 1)
                gla_keys(i)
                if i >= 2:
                    dve.wait_ge(sem("gla_acc"), i - 1)
                if i:
                    gla_acc(i - 1)
            cb = cum.rearrange("p (b s) -> p b s", s=P)
            tot = cb[:, :, P - 1:P]
            c4 = cum.rearrange("p (m t s) -> p m t s", t=NT, s=P)
            d1 = dl[1].rearrange("p m (t s) -> p m t s", s=P)
            d0 = dl[0].rearrange("p m (t s) -> p m t s", s=P)
            dve.wait_ge(sem("gla_q"), 6)
            dve.wait_ge(sem("gla_k"), 6)
            tt(dl[1].rearrange("p m (t s) -> p (m t) s", s=P), tot.to_broadcast([P, 2 * NT, P]), cb, ALU.subtract).then_inc(sem("gla_d"), 1)
            dve.wait_ge(sem("gla_acc"), nl - 1)
            gla_acc(nl - 1)
            dve.wait_ge(sem("gla_e"), 8)
            tt(gkx, gk, dl[1], ALU.mult).then_inc(sem("gla_kx"), 1)
            dve.wait_ge(sem("gla_kx"), 1)
            for m in range(2):
                last = tt(d1[:, m, 2:4, :], c4[:, m, 2:4, :], c4[:, m, 1:3, P - 1:P].to_broadcast([P, 2, P]), ALU.add)
            last.then_inc(sem("gla_d"), 1)
            dve.wait_ge(sem("gla_q"), 8)
            for m in range(2):
                last = tt(d0[:, m, 3, :], c4[:, m, 3, :], c4[:, m, 2, P - 1:P].to_broadcast([P, P]), ALU.add)
            link(last)
            for m in range(2):
                last = tt(d0[:, m, 3, :], d0[:, m, 3, :], c4[:, m, 1, P - 1:P].to_broadcast([P, P]), ALU.add)
            last.then_inc(sem("gla_d"), 1)
            dve.wait_ge(sem("gla_acc"), nl)
            gla_acc(nl)
            for h in range(4):
                dve.wait_ge(sem("gla_pv"), h + 1)
                dve.tensor_copy(gla_o[:, h, :], bank[h]).then_inc(sem("gla_oc"), 1)
            dve.wait_ge(sem("gog_silu"), 2)
            gn_split("gla", h_hi, h_lo, gog)
            for i in range(4):
                residual(at["wout1"], i, 1.0, 2)
            ffn("ffn2", GROUPS1, 2, True, 0.5, 3)

            dve.wait_ge(sem("p_hi"), 1)
            dve.tensor_tensor(h_lo[:, 0:2, :], psum[:, 6:8, :], h_hi[:, 0:2, :].bitcast(F32), ALU.subtract).then_inc(sem("p_lo"), 1)
            c = at["proj"]
            for i in range(4):
                dve.wait_ge(sem("pe_blk"), c + i + 1)
                for m in range(2):
                    last = dve.tensor_copy(emb[:, 2 * i + m, :], two(c + i, m))
                last.then_inc(sem("evac"), 1)
                lo(dve, c + 2 + i)
            dve.wait_ge(sem("p_in"), 32)
            dve.tensor_copy(buf_b[0:1, 1, :], arena[0:1, 1024:1536].bitcast(I32)).then_inc(sem("pos_f32"), 1)
            stats(3)
            c = at["gate"]
            for i in range(4):
                if i:
                    dve.wait_ge(sem("sig"), i)
                evac_scaled(c + i, buf_a)
                lo(dve, c + 2 + i)
            dve.wait_ge(sem("sig"), 4)
            angles(1)
            dve.wait_ge(sem("emb_rms"), 1)
            link(dve.reciprocal(buf_c[:, 1, :], buf_c[:, 1, :]))
            for t in range(KT):
                link(stt(buf_a[:, t % 2, :], emb[:, t, :], gains[:, G_PLE + t:G_PLE + t + 1], buf_c[:, 1, :], ALU.mult, ALU.mult))
                link(tt(buf_a[:, t % 2, :], buf_a[:, t % 2, :], sig[:, t, :], ALU.mult))
                tt(x_res[:, t, :], x_res[:, t, :], buf_a[:, t % 2, :], ALU.add).then_inc(sem("ple_x"), 1)
                if t:
                    fin(4, t - 1)
            fin(4, KT - 1)

            c = at["diff"]
            stats(4)
            for i in range(4):
                evac_scaled(c + i, q2[:, 2 * i:2 * i + 2, :])
                lo(dve, c + 2 + i)
            for i in range(4):
                evac_scaled(c + 4 + i, k2[:, 2 * i:2 * i + 2, :])
                lo(dve, c + 6 + i)
            for i in range(4):
                evac_tok(c + 8 + i, v2, i * BC)
                lo(dve, c + 10 + i)
            dve.wait_ge(sem("tables"), 2)
            gn_rope("dq")

            def pairs_attention(name, dsa):
                units = [(g, n) for g in range(KT) for n in range(NT)]

                def smax(u):
                    w, so = (units[u][1] + 1) * P, 16 * (u % 2)
                    dve.wait_ge(*use(name, "_s", u + 1))
                    dve.tensor_reduce(sm[:, so:so + 2], psum[:, 2 * (u % 2):2 * (u % 2) + 2, 0:w], AX.X, ALU.max,
                                      negate=True).then_inc(use(name, "_m")[0], 1)

                def norm(u):
                    w, so = (units[u][1] + 1) * P, 16 * (u % 2)
                    dve.wait_ge(*use(name, "_exp", u + 1))
                    link(dve.reciprocal(sm[:, so + 4:so + 6], sm[:, so + 2:so + 4]))
                    p0, p1 = (free_x[:, 2 * (u % 2) + cc, 0:w] for cc in range(2))
                    if dsa:
                        ts(p0, p0, sm[:, so + 4:so + 5], None, ALU.mult)
                        ts(p1, p1, sm[:, so + 5:so + 6], None, ALU.mult).then_inc(use(name, "_prob")[0], 1)
                    else:
                        d = free_x[:, 4 + u % 2, 0:w]
                        ts(p0, p0, sm[:, so + 4:so + 5], None, ALU.mult)
                        link(tt(sm[:, so + 5:so + 6], sm[:, so + 5:so + 6], gcol[:, 4:5], ALU.mult))
                        if u >= 2:
                            dve.wait_ge(*use(name, "_t", u - 1))
                        stt(d, p1, sm[:, so + 5:so + 6], p0, ALU.mult, ALU.add).then_inc(use(name, "_prob")[0], 1)

                def out_tile(g):
                    dve.wait_ge(*use(name, "_hi", g + 1))
                    tt(h_lo[:, g, :], bank[6 + g % 2], h_hi[:, g, :].bitcast(F32), ALU.subtract).then_inc(use(name, "_oc")[0], 1)

                smax(0)
                for u, (g, n) in enumerate(units):
                    if u + 1 < len(units):
                        smax(u + 1)
                    norm(u)
                    if dsa and n == 1 and g >= 1:
                        out_tile(g - 1)
                if dsa:
                    out_tile(KT - 1)

            pairs_attention("a2", False)
            gn_split("sub", h_hi, h_lo)
            for i in range(4):
                residual(at["wout2"], i, 1.0, 5)
            ffn("mlp0", GROUPS2, 5, False, 1.0, 6)

            c = at["dsa"]
            stats(6)
            evac_scaled(c, cq)
            lo(dve, c + 2)
            evac_scaled(c + 1, kw.unsqueeze(1), ms=(0,))
            lo(dve, c + 3)
            for i in range(4):
                evac_scaled(c + 2 + i, k2[:, 2 * i:2 * i + 2, :])
                lo(dve, c + 4 + i)
            for i in range(4):
                evac_tok(c + 6 + i, v2, i * BC)
                lo(dve, c + 8 + i)
            dve.wait_ge(sem("widx_t"), 1)
            dve.tensor_scalar(widx, bank[6].rearrange("p (n f) -> p n f", f=P)[:, :, HD:HD + 8],
                              (8 ** -0.5) * (HD ** -0.5), None, ALU.mult).then_inc(sem("widx_read"), 1)
            gn_split("cq", cq_hi, cq_lo)
            c = at["uq"]
            for i in range(6):
                dve.wait_ge(sem("pe_blk"), c + i + 1)
                dst = q2[:, 2 * i:2 * i + 2, :] if i < 4 else qi[:, 2 * i - 8:2 * i - 6, :]
                for m in range(2):
                    last = dve.tensor_copy(dst[:, m, :], two(c + i, m))
                last.then_inc(sem("evac"), 1)
                lo(dve, c + 2 + i)
            gn_rope("kx")
            for i in range(4):
                rope_out("qi", i, qi[:, i, :])

            u, rounds = 0, 0
            for n in range(1, NT):
                w = (n + 1) * P
                sc = buf_d[:, 0, 0:w]
                for hh in range(8):
                    dve.wait_ge(sem("dot_relu"), u + 1)
                    if hh == 0:
                        ts(sc, buf_c[:, u % 2, 0:w], widx[:, n, 0:1], None, ALU.mult).then_inc(sem("dot_acc"), 1)
                    else:
                        dve.wait_ge(sem("dot_acc"), u)
                        stt(sc, buf_c[:, u % 2, 0:w], widx[:, n, hh:hh + 1], sc, ALU.mult, ALU.add).then_inc(sem("dot_acc"), 1)
                    u += 1
                dve.wait_ge(sem("dot_acc"), u)
                link(tt(sc[:, n * P:], sc[:, n * P:], chunk_mask, ALU.add))
                for j in range(TOPK // 8):
                    dve.max(top8, sc).then_inc(sem("top8"), 1)
                    dve.wait_ge(sem("top8"), rounds + j + 1)
                    dve.match_replace(sc, top8, sc, -3e38).then_inc(sem("taken"), 1)
                    dve.wait_ge(sem("taken"), rounds + j + 1)
                rounds += TOPK // 8
                ts(kmask[:, n - 1, 0:w], sc, -2e38, -BIG, ALU.is_gt, ALU.mult).then_inc(sem("kmask_done"), 1)
                dve.wait_ge(sem("kmask_done"), n)
            gn_rope("sq")
            pairs_attention("a3", True)
            for i in range(4):
                residual(at["wout3"], i, 1.0, 7)
            ffn("mlp1", GROUPS2, 7, False, 1.0, None)
            for u in range(0, 2 * NT, 2):
                dve.wait_ge(sem("y_tr"), u + 1)
                if u:
                    dve.wait_ge(sem("y_copied"), u)
                n = u // 2
                dve.tensor_copy(arena[:, n * D:n * D + S], bank[4 + u % 4]).then_inc(sem("y_copied"), 1)

        @block.gpsimd
        def _(pool):
            def add_squares(ready, done, r0, d0, dst):
                for t in range(1, KT):
                    pool.wait_ge(sem(ready), r0 + t + 1)
                    if t == 1:
                        ins = pool.tensor_tensor(dst, sq[:, 0, :], sq[:, 1, :], ALU.add)
                    else:
                        pool.wait_ge(sem(done), d0 + t - 1)
                        ins = pool.tensor_tensor(dst, dst, sq[:, t % 2, :], ALU.add)
                    ins.then_inc(sem(done), 1)

            def fin(p):
                add_squares("sq_done", "ssq_done", 8 * p, 7 * p, ssq[:])

            def rope_cos(name, srcs, ready):
                for i, src in enumerate(srcs):
                    if ready:
                        pool.wait_ge(*use(name, ready, i + 1))
                    if i >= 2:
                        pool.wait_ge(*use(name, "_out", i - 1))
                    pool.tensor_tensor(buf_c[:, i % 2, :], src, cos_t[:], ALU.mult).then_inc(use(name, "_cos")[0], 1)

            def gn_cos(name):
                rope_cos(name, [buf_a[:, i % 2, :] for i in range(len(GN[name]["tiles"]))], "_nrm")

            def gla_q(i, src, dst, part=slice(0, S), e=None, s_=None):
                pool.wait_ge(sem("gla_e"), e)
                if s_:
                    pool.wait_ge(sem("gla_s"), s_)
                pool.tensor_tensor(dst[:, :, part], gq[:, :, part], src[:, :, part], ALU.mult).then_inc(sem("gla_q"), 1)

            fin(0)
            fin(1)
            pool.wait_ge(sem("tables"), 1)
            gn_cos("gq")
            for i in range(len(LEVELS)):
                gla_q(i, dl[i % 2], ql[i % 2], e=i + 1, s_=max(0, i - 1))
            gla_q(7, dl[0], ql[0], e=9, s_=7)
            gla_q(8, dl[1], ql[1], part=slice(256, 512), e=10, s_=6)
            gla_q(9, dl[0], dl[0], part=slice(384, 512), e=11)
            fin(2)
            fin(3)
            add_squares("emb_sq", "emb_ssq", 0, 0, buf_c[:, 0, :])
            fin(4)
            pool.wait_ge(sem("tables"), 2)
            gn_cos("dq")
            fin(5)
            fin(6)
            gn_cos("kx")
            pool.wait_ge(*use("kx", "_out", 1))
            pool.wait_ge(sem("evac"), at["uq"] + 6)
            rope_cos("qi", [qi[:, i, :] for i in range(4)], None)
            gn_cos("sq")
            fin(7)


INPUTS = ["x", "p", "ffn1_norm", "ffn1_w_gate", "ffn1_w_up", "ffn1_w_down", "mix_norm", "w_in", "q_norm", "k_norm",
          "attn_sinks", "gla_w_gate_up", "gla_b_gate", "gla_out_norm", "w_out", "ffn2_norm", "ffn2_w_gate", "ffn2_w_up",
          "ffn2_w_down", "ple_gate_norm", "ple_w_gate", "ple_w_proj", "ple_norm", "positions_2", "norm_mix_2",
          "norm_mlp_2", "mlp_w1_2", "mlp_w2_2", "diff_w_in_2", "diff_q_norm_2", "diff_k_norm_2", "diff_lam_q1_2",
          "diff_lam_k1_2", "diff_lam_q2_2", "diff_lam_k2_2", "diff_subln_2", "diff_w_out_2", "dsa_w_in_2",
          "dsa_cq_norm_2", "dsa_w_uq_2", "dsa_w_uq_idx_2", "dsa_q_norm_2", "dsa_k_norm_2", "dsa_w_out_2"]


def kernel(**inputs):
    import concourse.bacc as bacc
    from concourse.bass_utils import run_bass_kernel_spmd

    nc = bacc.Bacc("TRN2", target_bir_lowering=False, num_devices=1)
    arrays, io = {}, {}
    given = {name: np.ascontiguousarray(inputs[name]) for name in INPUTS}
    for name, a in {**given, **constants()}.items():
        arrays["in_" + name] = a
        io[name] = nc.dram_tensor("in_" + name, a.shape, mybir.dt.from_np(a.dtype), kind="ExternalInput").ap()
    out = nc.dram_tensor("out_0", (1, S, D), F32, kind="ExternalOutput").ap()
    program(nc, io, out)
    r = run_bass_kernel_spmd(nc, [arrays], core_ids=[0])
    return r.results[0]["out_0"]
```

```python
from contextlib import ExitStack
import math

import numpy as np
import concourse.bass as bass
from concourse import mybir

F32 = mybir.dt.float32
F32R = mybir.dt.float32r
BF16 = mybir.dt.bfloat16
I32 = mybir.dt.int32
U8 = mybir.dt.uint8
ALU = mybir.AluOpType
ACT = mybir.ActivationFunctionType
AX = mybir.AxisListType

P = 128
D = 1024
S = 512
KT = D // P
NT = S // P
BC = 256
EPS = 1e-6
BIG = 1e30
HD = 64
F1 = 2816
F2 = 4096
GROUPS1 = [8, 8, 6]
GROUPS2 = [8, 8, 8, 8]
TOPK = 128
LAM_INIT = 0.8 - 0.6 * math.exp(0.0)
LEVELS = [64, 32, 16, 8, 4, 2, 1]
TWO_PI = 2 * math.pi
ROUND = 1.5 * 2.0 ** 23

PAIR_UNITS = [(g, n) for g in range(KT) for n in (3, 1, 2, 0)]

G_FFN1, G_MIX, G_FFN2, G_PLEG, G_PLE, G_MIX0, G_MLP0, G_MIX1, G_MLP1 = range(0, 72, 8)
G_QN, G_KN, G_GLA, G_DQ, G_DK, G_SUB, G_SQ, G_SK, G_CQ, G_BG, G_LQ, G_LK, G_SINK = (
    72, 73, 74, 75, 76, 77, 78, 79, 80, 82, 84, 85, 86)
G_ROWS = 87
NORM_GAIN = [G_FFN1, G_MIX, G_FFN2, G_PLEG, G_MIX0, G_MLP0, G_MIX1, G_MLP1]


def constants():
    c = {}
    p = np.arange(P)
    c["c_ident"] = np.eye(P, dtype=np.float32)
    sel = np.zeros((P, 2 * KT + 2, 16), np.float32)
    for t in range(KT):
        sel[p, t, 2 * t + p // HD] = 1 / HD
        sel[:, KT + t, 2 * t:2 * t + 2] = 1 / P
    sel[:, 2 * KT:, 0:4] = 1 / 256
    c["c_sel"] = sel.reshape(P, -1)
    spread = np.zeros((P, KT * P), np.float32)
    spread[np.arange(KT * P) // HD, np.arange(KT * P)] = 1
    c["c_spread"] = spread
    rot1 = np.zeros((P, P), np.float32)
    rot2 = np.zeros((P, P), np.float32)
    for h0 in (0, HD):
        for rot, half in ((rot1, 32), (rot2, 8)):
            for i in range(half):
                rot[h0 + half + i, h0 + i] = -1
                rot[h0 + i, h0 + half + i] = 1
    c["c_rot"] = np.concatenate([rot1, rot2], 1)
    d = p % HD
    inv1 = np.power(np.float32(10000.0), -(2 * (d % 32)).astype(np.float32) / np.float32(64))
    inv2 = np.where(d < 16, np.power(np.float32(500000.0), -(2 * (d % 8)).astype(np.float32) / np.float32(16)), 0)
    c["c_inv"] = np.stack([inv1, inv2], 1).astype(np.float32)
    c["c_pos"] = np.arange(S, dtype=np.float32)[None]
    qi, kj = p[:, None], np.arange(2 * P)[None]
    rel = kj - P - qi
    band = np.where((rel <= 0) & (rel > -P), 0, -BIG).astype(np.float32)
    first = np.where(kj < P, -BIG, band).astype(np.float32)
    chunk = np.where((qi < 64) & (np.arange(P)[None] >= 64), -BIG, 0).astype(np.float32)
    c["c_mask"] = np.concatenate([band, first, chunk], 1)
    j, i = p[:, None], p[None]
    lev = [((i // s) % 2 == 1) & ((j // s) % 2 == 0) & (i // (2 * s) == j // (2 * s)) for s in LEVELS]
    lev.append(i == j)
    c["c_level"] = np.stack(lev, 1).astype(np.float32).reshape(P, -1)
    half = np.zeros((P, 2, P), np.float32)
    half[:64, 0] = 1
    half[64:, 1] = 1
    c["c_half"] = half.reshape(P, -1)
    return c


def plan():
    at, n = {}, 0
    for name, groups, per in (("ffn1", GROUPS1, 2), ("mix", None, 10), ("wout1", None, 4), ("ffn2", GROUPS1, 2),
                              ("proj", None, 4), ("gate", None, 4), ("diff", None, 12), ("wout2", None, 4),
                              ("mlp0", GROUPS2, 1), ("dsa", None, 16), ("wout3", None, 4),
                              ("mlp1", GROUPS2, 1)):
        if groups is None:
            at[name] = n
            n += per
        else:
            for g, tiles in enumerate(groups):
                at[name, g, "up"] = n
                n += per * tiles // 2
                at[name, g, "down"] = n
                n += 4
    at["end"] = n
    return at


def program(nc, io, out):
    at = plan()
    NB = at["end"]
    ctx = ExitStack()
    with ctx:
        def sb(name, shape, dt=F32):
            return ctx.enter_context(nc.sbuf_tensor(name, shape, dt))

        sems = {}

        def sem(name):
            if name not in sems:
                sems[name] = ctx.enter_context(nc.semaphore(name))
            return sems[name]

        x_res = sb("x_res", [P, KT, S])
        w_raw = sb("w_raw", [P, 2, KT * BC])
        w_hi = sb("w_hi", [P, 2, KT * BC], F32R)
        w_lo = sb("w_lo", [P, 2, KT * BC], F32R)
        base = nc.sbuf_base() if callable(nc.sbuf_base) else nc.sbuf_base
        region = sb("region", [P, 4 * KT + 4, S])
        region_at = base
        KB = KT * S * 4

        def alias(name, shape, dt, offset):
            return nc.alloc_sbuf_tensor_at(name, shape, dt, offset=region_at + offset)

        xg_hi = alias("xg_hi", [P, KT, S], F32R, 0)
        xg_lo = alias("xg_lo", [P, KT, S], F32R, KB)
        h_hi = alias("h_hi", [P, KT, S], F32R, 2 * KB)
        h_lo = alias("h_lo", [P, KT, S], F32R, 3 * KB)
        free_x = alias("free_x", [P, 2 * KT, S], F32, 0)
        kmask = alias("kmask", [P, NT - 1, S], BF16, 12 * S * 4)
        free_h = alias("free_h", [P, 2 * KT, S], F32, 2 * KB)

        level = alias("level", [P, 8, P], U8, 2 * KB + 14 * S * 4)
        wgu = alias("wgu", [16, 256], F32, 2 * KB + 15 * S * 4)

        rstd = alias("rstd", [P, S], F32, 4 * KB)
        rstd_tok = sb("rstd_tok", [P, NT])
        buf_a = sb("buf_a", [P, 2, S])
        buf_b = sb("buf_b", [P, 2, S])
        buf_c = sb("buf_c", [P, 2, S])
        buf_d = sb("buf_d", [P, 2, S])
        ssq = alias("ssq", [P, S], F32, 4 * KB + S * 4)
        sq = alias("sq", [P, 2, S], F32, 4 * KB + 2 * S * 4)
        rs_hi = [alias(f"rs_hi{i}", [P, S], F32R, 4 * KB + (1 - i) * S * 4) for i in range(2)]
        rs_lo = [alias(f"rs_lo{i}", [P, S], F32R, 4 * KB + (2 + i) * S * 4) for i in range(2)]
        cos_t = sb("cos_t", [P, S])
        sin_t = sb("sin_t", [P, S])
        arena = sb("arena", [P, 10752])
        gains = sb("gains", [P, G_ROWS])
        gcol = sb("gcol", [P, 8])
        ident = sb("ident", [P, P])
        ident_bf = sb("ident_bf", [P, P], BF16)
        sel = sb("sel", [P, 2 * KT + 2, 16])
        spread = sb("spread", [P, KT * P], F32R)
        rot = sb("rot", [P, 2, P])
        inv = sb("inv", [P, 2])
        mask_bf = sb("mask_bf", [P, 5 * P], BF16)
        mean = sb("mean", [P, P])
        eps = sb("eps", [P, 1])
        one = sb("one", [P, 1])
        sm = sb("sm", [P, 96])

        psum = ctx.enter_context(nc.psum_tensor("psum", [P, 8, S], F32))
        bank = [psum[:, i, :] for i in range(8)]

        TILES = {"gq": 5, "gla": 4, "dq": 16, "sub": 8, "cq": 2, "kx": 1, "qi": 4, "sq": 16}
        ROPE, SPLIT, NORM = ("gq", "dq", "kx", "qi", "sq"), ("gla", "sub", "cq"), tuple(t for t in TILES if t != "qi")

        def use(name, kind, v=0):
            if name in ("a2", "a3"):
                per = {"_oc": KT, "_hi": 0}.get(kind, KT * NT)
                return sem("pairs" + kind), v + (per if name == "a3" else 0)
            users = (NORM if kind in ("_sq", "_msq", "_bc", "_nrm", "_rms", "_rs") else
                     ROPE if kind in ("_rot", "_sin", "_cos") else
                     SPLIT if kind == "_hi" else ("gla",) if kind == "_pre" else tuple(TILES))
            each = (lambda n: 1) if kind in ("_rms", "_rs") else TILES.get
            return sem("norm" + kind), v + sum(each(n) for n in users[:users.index(name)])

        def rows(w, k0, nk):
            return w[P * k0:P * (k0 + nk), :].rearrange("(k p) f -> p k f", p=P)

        def wait_lo(e, c, j=0):
            e.wait_ge(sem("lo_done"), 2 * j + (c + 1))

        def load(e, c, j, src, nk=KT, cols=BC):
            if c >= 2 or not isinstance(j, int):
                e.wait_ge(sem("lo_done"), 2 * j + (c - 1))
            dst = w_raw[:, c % 2, :].rearrange("p (k f) -> p k f", f=BC)[:, 0:nk, 0:cols]
            e.dma_start(dst, src).then_inc(sem(f"landed{c % 2}"), 16)

        def used(c):
            for name, off, n in (("proj", 0, 4), ("dsa", 4, 2), ("dsa", 8, 4)):
                if 0 <= c - at[name] - off < n:
                    return 2 * BC
            return KT * BC

        def hi(e, c, j=0):
            if c >= NB:
                return
            e.wait_ge(sem(f"landed{c % 2}"), 16 * j + 16 * (c // 2 + 1))
            if c >= 2:
                e.wait_ge(sem("pe_blk"), 2 * j + (c - 1))
            n = used(c)
            e.activation(w_hi[:, c % 2, 0:n], w_raw[:, c % 2, 0:n], ACT.Copy).then_inc(sem("hi_done"), 1)

        def lo(e, c, j=0):
            if c >= NB:
                return
            e.wait_ge(sem("hi_done"), 2 * j + (c + 1))
            n = used(c)
            e.tensor_tensor(w_lo[:, c % 2, 0:n], w_raw[:, c % 2, 0:n], w_hi[:, c % 2, 0:n].bitcast(F32),
                            ALU.subtract).then_inc(sem("lo_done"), 1)

        def two(c, m):
            return bank[2 * (c % 2) + m]

        block = ctx.enter_context(nc.Block())

        @block.sync
        def _(sp):
            tok = io["x"].rearrange("a (n p) d -> p (a n) d", p=P)
            xin = arena[:, 0:4096].rearrange("p (n d) -> p n d", n=NT)
            stack = buf_d[:, 0, 0:P]
            sp.wait_ge(sem("zeroed"), 1)
            n_rows = 0

            def row(r, src):
                nonlocal n_rows
                n_rows += 1
                sp.dma_start(stack[r:r + src.shape[0], 0:src.shape[1]], src).then_inc(sem("gain_rows"), 16)

            def as_rows(v):
                return v.rearrange("a (k p) -> (a k) p", p=P)

            row(G_FFN1, as_rows(io["ffn1_norm"]))
            sp.dma_start(ident[:], io["c_ident"]).then_inc(sem("const_a"), 16)
            for n in range(NT):
                sp.dma_start(xin[:, n, :], tok[:, n, :]).then_inc(sem("x_in"), 16)
            for g, name in ((G_MIX, "mix_norm"), (G_FFN2, "ffn2_norm"), (G_PLEG, "ple_gate_norm"), (G_PLE, "ple_norm"),
                            (G_GLA, "gla_out_norm"), (G_SUB, "diff_subln_2"), (G_CQ, "dsa_cq_norm_2"), (G_BG, "gla_b_gate")):
                row(g, as_rows(io[name]))
            for i, (ga, gb) in enumerate(((G_MIX0, G_MLP0), (G_MIX1, G_MLP1))):
                row(ga, as_rows(io["norm_mix_2"][i:i + 1, :]))
                row(gb, as_rows(io["norm_mlp_2"][i:i + 1, :]))
            for g, name in ((G_QN, "q_norm"), (G_KN, "k_norm"), (G_DQ, "diff_q_norm_2"), (G_DK, "diff_k_norm_2"),
                            (G_SQ, "dsa_q_norm_2"), (G_SK, "dsa_k_norm_2")):
                for half in range(2):
                    n_rows += 1
                    sp.dma_start(stack[g:g + 1, HD * half:HD * half + HD], io[name]).then_inc(sem("gain_rows"), 16)
            for g, names in ((G_LQ, ("diff_lam_q1_2", "diff_lam_q2_2")), (G_LK, ("diff_lam_k1_2", "diff_lam_k2_2"))):
                for half in range(2):
                    n_rows += 1
                    sp.dma_start(stack[g:g + 1, HD * half:HD * half + HD], io[names[half]]).then_inc(sem("gain_rows"), 16)
            row(G_SINK, io["attn_sinks"])
            assert n_rows == 30
            load(sp, 0, 0, rows(io["ffn1_w_gate"][0], 0, KT)[:, :, 0:BC])
            load(sp, 1, 0, rows(io["ffn1_w_up"][0], 0, KT)[:, :, 0:BC])
            sp.dma_start(sel[:].rearrange("p t c -> p (t c)"), io["c_sel"]).then_inc(sem("const_b"), 16)
            sp.dma_start(rot[:].rearrange("p a c -> p (a c)"), io["c_rot"]).then_inc(sem("const_b"), 16)
            sp.dma_start(inv[:], io["c_inv"]).then_inc(sem("const_b"), 16)
            sp.wait_ge(sem("x_copied"), KT)
            sp.dma_start(arena[:, 0:5 * P], io["c_mask"]).then_inc(sem("const_c"), 16)
            sp.dma_start(arena[0:1, 1024:1536], io["c_pos"]).then_inc(sem("const_c"), 16)
            sp.dma_start(arena[:, 2048:2304], io["c_half"]).then_inc(sem("const_c"), 16)
            sp.dma_start(arena[:, 3072:4096], io["c_spread"]).then_inc(sem("const_c"), 16)

            def ffn(name, groups, wg, wu, wd, skip=0):
                f0 = 0
                for g, tiles in enumerate(groups):
                    c = at[name, g, "up"]
                    if wg is not None:
                        vg, vu = rows(wg, 0, KT), rows(wu, 0, KT)
                        with sp.Fori(1 if g == 0 and skip else 0, tiles // 2) as j:
                            load(sp, c, j, vg[:, :, bass.ds(j * BC + P * f0, BC)])
                            load(sp, c + 1, j, vu[:, :, bass.ds(j * BC + P * f0, BC)])
                    else:
                        vu = rows(wu, 0, KT)
                        with sp.Fori(0, tiles // 4) as j:
                            for s in range(2):
                                load(sp, c + s, j, vu[:, :, bass.ds(j * 2 * BC + (P * f0 + s * BC), BC)])
                    c = at[name, g, "down"]
                    vd = rows(wd, f0, tiles)
                    with sp.Fori(0, 2) as j:
                        for s in range(2):
                            load(sp, c + s, j, vd[:, :, bass.ds(j * 2 * BC + s * BC, BC)], nk=tiles)
                    f0 += tiles

            ffn("ffn1", GROUPS1, io["ffn1_w_gate"][0], io["ffn1_w_up"][0], io["ffn1_w_down"][0], skip=1)
            c, v = at["mix"], rows(io["w_in"][0], 0, KT)
            for i, (f0, cols) in enumerate(((0, 256), (256, 256), (512, 256), (1792, 16), (768, 256), (1024, 256),
                                            (1280, 256), (1536, 256), (1808, 256), (2064, 256))):
                load(sp, c + i, 0, v[:, :, f0:f0 + cols], cols=cols)
                if i == 3:
                    sp.wait_ge(sem("pe_blk"), at["mix"])
                    sp.dma_start(wgu[:], io["gla_w_gate_up"][0]).then_inc(sem("mix_const"), 16)
                    sp.dma_start(free_h[:, 12:14, :].rearrange("p a c -> p (a c)"), io["c_level"]).then_inc(sem("mix_const"), 16)

            def plain(name, w, nblocks, nk=KT, off=0, first=0):
                c, v = at[name] + off, rows(w, 0, nk)
                for i in range(first, nblocks):
                    load(sp, c + i, 0, v[:, :, i * BC:(i + 1) * BC], nk=nk)

            plain("wout1", io["w_out"][0], 2)
            kk, kswap = arena[:, 2048:2560], arena[:, 2560:3072]
            sp.wait_ge(*use("gq", "_out", 5))
            sp.dma_start(kswap[0:HD, :], kk[HD:P, :]).then_inc(sem("kswap"), 16)
            sp.dma_start(kswap[HD:P, :], kk[0:HD, :]).then_inc(sem("kswap"), 16)
            plain("wout1", io["w_out"][0], 4, first=2)
            sp.wait_ge(sem("pe_blk"), at["wout1"] + 1)
            sp.dma_start(arena[:, 0:1024].rearrange("p (n d) -> p n d", n=NT),
                         io["p"].rearrange("l a (n p) d -> p (l a n) d", p=P)).then_inc(sem("p_in"), 16)
            sp.dma_start(arena[0:1, 1024:1536].bitcast(I32), io["positions_2"]).then_inc(sem("p_in"), 16)
            ffn("ffn2", GROUPS1, io["ffn2_w_gate"][0], io["ffn2_w_up"][0], io["ffn2_w_down"][0])
            plain("proj", io["ple_w_proj"][0], 4, nk=2)
            plain("gate", io["ple_w_gate"][0], 4)
            plain("diff", io["diff_w_in_2"][0], 12)
            plain("wout2", io["diff_w_out_2"][0], 4)
            ffn("mlp0", GROUPS2, None, io["mlp_w1_2"][0], io["mlp_w2_2"][0])
            c, v = at["dsa"], rows(io["dsa_w_in_2"][0], 0, KT)
            uq, uqi = rows(io["dsa_w_uq_2"][0], 0, 2), rows(io["dsa_w_uq_idx_2"][0], 0, 2)
            k0, v0 = 256, 1280
            ki = arena[:, 10240:10752]
            dsa_blocks = ([(v, 0, 256, KT), (v, 2304, 72, KT), (v, k0, BC, KT), (v, k0 + BC, BC, KT), (uqi, 0, BC, 2),
                           (uqi, BC, BC, 2), (v, k0 + 2 * BC, BC, KT), (v, k0 + 3 * BC, BC, KT)]
                          + [(uq, i * BC, BC, 2) for i in range(4)] + [(v, v0 + i * BC, BC, KT) for i in range(4)])
            for i, (w, f0, cols, nk) in enumerate(dsa_blocks):
                load(sp, c + i, 0, w[:, :, f0:f0 + cols], nk=nk, cols=cols)
                if i == 8:
                    sp.wait_ge(*use("kx", "_out", 1))
                    sp.dma_start(ki[HD:P, :], ki[0:HD, :]).then_inc(sem("kswap"), 16)
            plain("wout3", io["dsa_w_out_2"][0], 2)
            plain("wout3", io["dsa_w_out_2"][0], 4, first=2)
            ffn("mlp1", GROUPS2, None, io["mlp_w1_2"][1], io["mlp_w2_2"][1])
            tok_out = out.rearrange("a (n p) d -> p (a n) d", p=P)
            y = arena[:, 0:4096].rearrange("p (n d) -> p n d", n=NT)
            for n in range(NT):
                sp.wait_ge(sem("y_copied"), 2 * (n + 1))
                sp.dma_start(tok_out[:, n, :], y[:, n, :]).then_inc(sem("stored"), 16)
            sp.wait_ge(sem("stored"), 16 * NT)


        rs16 = [ssq[0:16, :], rstd[0:16, :]]
        aq = arena[:, 0:2048].rearrange("p (k t) -> p k t", t=S)
        ak = arena[:, 2048:2560]
        ak_swap = arena[:, 2560:3072]
        av = arena[:, 3072:3584].rearrange("p (n f) -> p n f", n=NT)
        gq = arena[:, 3584:4608].rearrange("p (k t) -> p k t", t=S)
        gk = arena[:, 4608:5632].rearrange("p (k t) -> p k t", t=S)
        gv = arena[:, 5632:7680].rearrange("p (n f) -> p n f", n=NT)
        gog = arena[:, 7680:9728].rearrange("p (k t) -> p k t", t=S)
        cum = arena[:, 9728:10752]
        glr = ssq[0:16, :]
        emb = arena[:, 1536:5632].rearrange("p (k t) -> p k t", t=S)
        sig = arena[:, 5632:9728].rearrange("p (k t) -> p k t", t=S)
        k2 = arena[:, 0:4096].rearrange("p (k t) -> p k t", t=S)
        v2 = arena[:, 4096:8192].rearrange("p (n f) -> p n f", n=NT)
        q2 = free_h[:, 0:KT, :]
        qi = arena[:, 8192:10240].rearrange("p (k t) -> p k t", t=S)
        ki = arena[:, 10240:10752]
        cq_hi, cq_lo = h_lo[:, 0:2, :], h_lo[:, 2:4, :]
        cq = free_h[:, 12:14, :]
        kw = free_h[:, 14, :]
        index_score = [None, free_h[:, 15, :], buf_d[:, 0, :], buf_d[:, 1, :]]
        acc_at = free_x[:, 0:4, :].rearrange("p h (t i) -> p h t i", i=P)
        cross_at = free_x[:, 4:10, :].rearrange("p a (b i) -> p (a b) i", i=P)
        gkx = free_x[:, 14:16, :]
        gla_o = free_x[:, 10:14, :]
        ql = [buf_a[:, :, :], free_x[:, 10:12, :]]
        kl = [buf_b[:, :, :], free_x[:, 12:14, :]]
        dl = [buf_c[:, :, :], buf_d[:, :, :]]
        band_mask, first_mask, chunk_mask = mask_bf[:, 0:256], mask_bf[:, 256:512], mask_bf[:, 512:640]
        widx = sm[:, 32:64].rearrange("p (n h) -> p n h", n=NT)
        sinks = sm[:, 88:96]
        top8 = sm[:, 80:88]
        GN = {
            "gq": dict(tiles=[(aq[:, t, :], aq[:, t, :], 0, t, gcol[:, 0:1]) for t in range(4)]
                       + [(ak, ak, 0, 4, gains[:, G_KN:G_KN + 1])], sel=0, sizes=[5]),
            "dq": dict(tiles=[(q2[:, t, :], q2[:, t, :], 0, t, gcol[:, 1:2]) for t in range(KT)]
                       + [(k2[:, t, :], k2[:, t, :], 1, t, gains[:, G_DK:G_DK + 1]) for t in range(KT)], sel=0, sizes=[8, 8]),
            "kx": dict(tiles=[(kw, ki, 0, 0, None)], sel=0, sizes=[1]),
            "sq": dict(tiles=[(k2[:, t, :], k2[:, t, :], 1, t, gains[:, G_SK:G_SK + 1]) for t in range(KT)]
                       + [(q2[:, t, :], q2[:, t, :], 0, t, gcol[:, 2:3]) for t in range(KT)], sel=0, sizes=[8, 8]),
            "gla": dict(tiles=[(gla_o[:, t, :], 4 + t, 0, t, gains[:, G_GLA:G_GLA + 1]) for t in range(4)], sel=1, sizes=[4]),
            "sub": dict(tiles=[(q2[:, t, :], t, 0, t, gcol[:, 3:4]) for t in range(KT)], sel=1, sizes=[8]),
            "cq": dict(tiles=[(cq[:, t, :], t, 0, t, gains[:, G_CQ + t:G_CQ + t + 1]) for t in range(2)], sel=2, sizes=[2]),
        }

        def ngain(p, t):
            g = NORM_GAIN[p] + t
            return gains[:, g:g + 1]

        @block.tensor
        def _(pe):
            def mm(out, lhsT, rhs, start=True, stop=True):
                return pe.matmul(out, lhsT, rhs, start=start, stop=stop)

            def mm3(out, w, a, first, last):
                mm(out, w[0], a[0], first, False)
                mm(out, w[0], a[1], False, False)
                return mm(out, w[1], a[0], False, last)

            def begin(c, j=0):
                wait_lo(pe, c, j)
                if c >= 2 or not isinstance(j, int):
                    pe.wait_ge(sem("evac"), 2 * j + (c - 1))

            def wtile(c, k, m, width=P):
                at0 = k * BC + m * P
                return w_hi[:, c % 2, at0:at0 + width], w_lo[:, c % 2, at0:at0 + width]

            def blk(c, j=0, a=(xg_hi, xg_lo), nk=KT, ms=(0, 1), waits={}, after=None):
                begin(c, j)
                for k in range(nk):
                    for s_, v in waits.get(k, ()):
                        pe.wait_ge(s_, v)
                    for m in ms:
                        last = mm3(two(c, m), wtile(c, k, m), (a[0][:, k, :], a[1][:, k, :]), k == 0, k == nk - 1)
                    if k == nk - 1:
                        last.then_inc(sem("pe_blk"), 1)
                    if after:
                        after(k)

            def tok_part(c, m, width, per_bank, after=None):
                for t in range(NT):
                    dst = two(c, m + t // per_bank)[:, (t % per_bank) * width:(t % per_bank + 1) * width]
                    ts = slice(t * P, (t + 1) * P)
                    for k in range(KT):
                        last = mm3(dst, (xg_hi[:, k, ts], xg_lo[:, k, ts]), wtile(c, k, m, width), k == 0, k == KT - 1)
                    if t == NT - 1:
                        last.then_inc(sem("pe_blk"), 1)
                    if after:
                        after(t)

            def tok_blk(c, after=None):
                begin(c)
                tok_part(c, 0, BC, 2, after)

            def xg_waits(p):
                return {k: [(sem("xg_done"), 8 * p + k + 1)] for k in range(KT)}

            def stats(p):
                pe.wait_ge(sem("ssq_done"), 7 * (p + 1))
                last = mm(bank[4], mean[:], ssq[:])
                if p in (1, 4, 6):
                    for t in range(NT):
                        last = mm(bank[5][:, t:t + 1], ssq[:, t * P:(t + 1) * P], mean[:, 0:1])
                last.then_inc(sem("ms"), 1)

            hcount = [0]

            def ffn(name, groups, p, gated, between=None):
                for g, tiles in enumerate(groups):
                    c, nb = at[name, g, "up"], tiles if gated else tiles // 2
                    if g == 0:
                        blk(c, waits=xg_waits(p))
                        stats(p)
                        blk(c + 1)
                    with pe.Fori(1 if g == 0 else 0, nb // 2) as j:
                        blk(c, j)
                        blk(c + 1, j)
                    h0 = hcount[0]
                    hcount[0] += tiles // 2
                    waits = {0: [(sem("h_done"), h0 + tiles // 2 - 1)], tiles - 2: [(sem("h_done"), h0 + tiles // 2)]}
                    c = at[name, g, "down"]
                    with pe.Fori(0, 2) as j:
                        for s in range(2):
                            blk(c + s, j, (h_hi, h_lo), tiles, waits=waits)
                    if between and g == 0:
                        between()

            def gn_stats(name, part=None):
                d = GN[name]
                for i in part or range(len(d["tiles"])):
                    z, o, grp, idx, g = d["tiles"][i]
                    pe.wait_ge(*use(name, "_sq", i + 1))
                    mm(bank[4 + grp][0:16, :], sel[:, d["sel"] * KT + idx, :], sq[:, i % 2, :], idx == 0,
                       idx == d["sizes"][grp] - 1).then_inc(use(name, "_msq")[0], 1)

            def rotate(name, rope, i):
                pe.wait_ge(*use(name, "_nrm", i + 1))
                if i >= 2:
                    pe.wait_ge(*use(name, "_sin", i - 1))
                mm(bank[4 + i % 2], rot[:, rope, :], buf_a[:, i % 2, :]).then_inc(use(name, "_rot")[0], 1)

            def gn_step(name, rope, i):
                z, o, grp, idx, g = GN[name]["tiles"][i]
                if i == 0:
                    pe.wait_ge(*use(name, "_rs", 1))
                if i >= 2:
                    pe.wait_ge(*use(name, "_nrm", i - 1))
                mm(bank[6 + i % 2], spread[:, idx * P:(idx + 1) * P], rs_hi[grp][:], True, False)
                mm(bank[6 + i % 2], spread[:, idx * P:(idx + 1) * P], rs_lo[grp][:], False, True).then_inc(use(name, "_bc")[0], 1)
                if rope is not None and i >= 1:
                    rotate(name, rope, i - 1)

            def gn_apply(name, rope, first=0):
                for i in range(first, len(GN[name]["tiles"])):
                    gn_step(name, rope, i)
                if rope is not None:
                    rotate(name, rope, len(GN[name]["tiles"]) - 1)

            pe.wait_ge(sem("const_a"), 16)
            pe.wait_ge(sem("gain_rows"), 16 * 30)
            pe.transpose(bank[7][:, 0:G_ROWS], buf_d[0:G_ROWS, 0, 0:P], ident[0:G_ROWS, 0:G_ROWS]).then_inc(sem("gains_t"), 1)
            pe.wait_ge(sem("x_in"), 16 * NT)
            for k in range(KT):
                if k >= 3:
                    pe.wait_ge(sem("x_copied"), k - 2)
                for n in range(NT):
                    last = pe.transpose(bank[4 + k % 3][:, n * P:(n + 1) * P],
                                        arena[:, n * D + k * P:n * D + (k + 1) * P], ident[:])
                last.then_inc(sem("x_tr"), 1)

            def setup():
                pe.wait_ge(sem("const_c"), 64)
                mm(bank[7], mean[0:1, :], arena[0:1, 1024:1536]).then_inc(sem("pos_mm"), 1)
                pe.wait_ge(sem("lam_prod"), 1)
                mm(bank[6][:, 0:1], arena[:, 2048:2176], sm[:, 64:65])
                mm(bank[6][:, 1:2], arena[:, 2176:2304], sm[:, 64:65])
                mm(bank[6][:, 8:16], mean[0:8, :], sm[0:8, 66:74]).then_inc(sem("lam_mm"), 1)

            ffn("ffn1", GROUPS1, 0, True, between=setup)

            c = at["mix"]
            blk(c, waits=xg_waits(1))
            stats(1)
            blk(c + 1)
            gn_stats("gq", (0, 1))
            begin(c + 2)
            for k in range(KT):
                mm3(two(c + 2, 0), wtile(c + 2, k, 0), (xg_hi[:, k, :], xg_lo[:, k, :]), k == 0, k == KT - 1)
            tok_part(c + 2, 1, P, 4)
            gn_stats("gq", (2, 3))
            blk(c + 3, ms=(0,))
            gn_stats("gq", (4,))
            blk(c + 4)
            pe.wait_ge(sem("evac"), c + 4)
            pe.wait_ge(sem("mix_const"), 32)
            for m in range(2):
                mm(bank[6 + m], wgu[:, m * P:(m + 1) * P], glr).then_inc(sem("gate_mm"), 1)
            blk(c + 5)
            pe.wait_ge(sem("gate_read"), 1)
            tok_blk(c + 6, after=lambda t: gn_step("gq", 0, t))
            tok_blk(c + 7, after=lambda t: gn_step("gq", 0, 4) if t == 0 else rotate("gq", 0, 4) if t == 1 else None)
            blk(c + 8)
            blk(c + 9)

            pe.wait_ge(sem("evac"), c + 10)
            pe.wait_ge(*use("gq", "_out", 5))
            pe.wait_ge(sem("kswap"), 32)

            def a1_scores(h):
                half, kv = h % 2, h // 4
                hs = slice(HD * half, HD * half + HD)
                keys = ak if half == kv else ak_swap
                if h >= 2:
                    pe.wait_ge(sem("a1_exp"), h - 1)
                for n in range(NT):
                    dst = bank[2 * (h % 2) + n // 2][:, (n % 2) * 256:(n % 2 + 1) * 256]
                    mm(dst, ident_bf[:], first_mask if n == 0 else band_mask, True, False)
                    q = aq[hs, h // 2, n * P:(n + 1) * P]
                    if n == 0:
                        last = mm(dst[:, P:], q, keys[hs, 0:P], False, True)
                    else:
                        last = mm(dst, q, keys[hs, (n - 1) * P:(n + 1) * P], False, True)
                last.then_inc(sem("a1_s"), 1)

            def a1_pt(h):
                return free_x[:, 6 + 2 * (h % 2):8 + 2 * (h % 2), :].rearrange("p a (b q) -> p (a b) q", q=P)

            def a1_p(h):
                return free_x[:, 2 * (h % 3):2 * (h % 3) + 2, :].rearrange("p a (b q) -> p (a b) q", q=P)

            def a1_transpose(h):
                pe.wait_ge(sem("a1_prob"), h + 1)
                if h >= 1:
                    pe.wait_ge(sem("a1_ptc"), h)
                for i in range(2 * NT):
                    last = pe.transpose(bank[4 + i // 4][:, (i % 4) * P:(i % 4 + 1) * P], a1_p(h)[:, i, :], ident[:])
                last.then_inc(sem("a1_t"), 1)

            def a1_values(h):
                t, hs, kv = h // 2, slice(HD * (h % 2), HD * (h % 2) + HD), h // 4
                pe.wait_ge(sem("a1_ptc"), h + 1)
                if t >= 2:
                    pe.wait_ge(sem("a1_out"), t - 1)
                for n in range(NT):
                    for w in ((1,) if n == 0 else (0, 1)):
                        last = mm(bank[6 + t % 2][hs, n * P:(n + 1) * P], av[:, n - 1 + w, kv * HD:(kv + 1) * HD],
                                  a1_pt(h)[:, 2 * n + w, :], w == 0 or n == 0, w == 1)
                last.then_inc(sem("a1_pv"), 1)

            a1_scores(0)
            a1_scores(1)
            for h in range(8):
                if h < 6:
                    a1_scores(h + 2)
                a1_transpose(h)
                if h >= 1:
                    a1_values(h - 1)
            a1_values(7)

            def gla_pairs(base_bank, kmat, qmat, dq, name):
                for h in range(4):
                    hs = slice(HD * (h % 2), HD * (h % 2) + HD)
                    for J in range(NT - dq):
                        last = mm(bank[base_bank + h][:, J * P:(J + 1) * P],
                                  kmat[hs, h // 2, J * P:(J + 1) * P], qmat[hs, h // 2, (J + dq) * P:(J + dq + 1) * P])
                last.then_inc(sem(name), 1)

            pe.wait_ge(sem("a1_out"), 4)
            for i in range(len(LEVELS)):
                pe.wait_ge(sem("gla_k"), i + 1)
                pe.wait_ge(sem("gla_q"), i + 1)
                if i >= 2:
                    pe.wait_ge(sem("gla_acc"), i - 1)
                gla_pairs(4 * (i % 2), kl[i % 2], ql[i % 2], 0, "gla_s")
            i = len(LEVELS)
            pe.wait_ge(sem("gla_acc"), i - 1)
            gla_pairs(4 * (i % 2), gk, gq, 0, "gla_s")
            pe.wait_ge(sem("gla_kx"), 1)
            pe.wait_ge(sem("gla_q"), len(LEVELS) + 1)
            pe.wait_ge(sem("gla_acc"), len(LEVELS))
            gla_pairs(0, gkx, ql[0], 1, "gla_x")
            pe.wait_ge(sem("gla_acc"), len(LEVELS) + 1)
            pe.wait_ge(sem("gla_q"), len(LEVELS) + 2)
            gla_pairs(4, gkx, ql[1], 2, "gla_x")
            pe.wait_ge(sem("gla_q"), len(LEVELS) + 3)
            pe.wait_ge(sem("gla_xc"), 1)
            gla_pairs(0, gkx, dl[0], 3, "gla_x")
            pe.wait_ge(sem("gla_xc"), 3)
            xoff = {1: 0, 2: 12, 3: 20}
            for h in range(4):
                for I in range(NT):
                    for J in range(I + 1):
                        a = acc_at[:, h, I, :] if I == J else cross_at[:, xoff[I - J] + h * (NT - I + J) + J, :]
                        last = mm(bank[h][:, I * P:(I + 1) * P], gv[:, J, h * P:(h + 1) * P], a, J == 0, J == I)
                last.then_inc(sem("gla_pv"), 1)
            gn_stats("gla")
            gn_apply("gla", None)

            def wout(name, waits):
                for i in range(4):
                    blk(at[name] + i, a=(h_hi, h_lo), waits=waits if i == 0 else {})

            wout("wout1", {4 + i: [use("gla", "_out", i + 1)] for i in range(4)})
            ffn("ffn2", GROUPS1, 2, True)

            pe.wait_ge(sem("p_in"), 32)
            for k in range(2):
                for n in range(NT):
                    last = pe.transpose(bank[6 + k][:, n * P:(n + 1) * P], arena[:, n * 256 + k * P:n * 256 + (k + 1) * P], ident[:])
                last.then_inc(sem("p_tr"), 1)
            pe.wait_ge(sem("p_lo"), 1)
            for i in range(4):
                blk(at["proj"] + i, a=(h_hi, h_lo), nk=2)
            blk(at["gate"], waits=xg_waits(3))
            stats(3)
            pe.wait_ge(sem("emb_ssq"), 7)
            mm(bank[5], mean[:], buf_c[:, 0, :]).then_inc(sem("emb_ms"), 1)
            pe.wait_ge(sem("pos_f32"), 1)
            mm(bank[7], mean[0:1, :], buf_b[0:1, 1, :]).then_inc(sem("pos_mm"), 1)
            for i in range(1, 4):
                blk(at["gate"] + i)

            c = at["diff"]
            blk(c, waits=xg_waits(4))
            stats(4)
            for i in range(1, 8):
                blk(c + i)
                gn_stats("dq", (2 * i - 2, 2 * i - 1))
            tok_blk(c + 8, after=lambda t: gn_stats("dq", (14, 15)) if t == 0 else None)
            for i in range(3):
                tok_blk(c + 9 + i, after=lambda t: gn_step("dq", 1, 4 * i + t))
            gn_apply("dq", 1, first=12)

            def pairs_attention(name, dsa):
                units = PAIR_UNITS

                def scores(u):
                    g, n = units[u]
                    w = (n + 1) * P
                    if u >= 2:
                        pe.wait_ge(*use(name, "_exp", u - 1))
                    for cc in range(2):
                        hs = slice(HD * cc, HD * cc + HD)
                        dst = bank[2 * (u % 2) + cc]
                        mm(dst[:, 0:w], q2[hs, g, n * P:(n + 1) * P], k2[hs, g, 0:w], True, False)
                        if dsa and n:
                            last = mm(dst[:, 0:w], ident_bf[:], kmask[:, n - 1, 0:w], False, True)
                        else:
                            last = mm(dst[:, n * P:w], ident_bf[:], chunk_mask, False, True)
                    last.then_inc(use(name, "_s")[0], 1)

                def transposes(u):
                    g, n = units[u]
                    pe.wait_ge(*use(name, "_prob", u + 1))
                    if dsa:
                        if u >= 1:
                            pe.wait_ge(*use(name, "_ptc", u))
                        for cc in range(2):
                            for J in range(n + 1):
                                last = pe.transpose(bank[4 + cc][:, J * P:(J + 1) * P],
                                                    free_x[:, 2 * (u % 3) + cc, J * P:(J + 1) * P], ident[:])
                    else:
                        if u >= 2:
                            pe.wait_ge(*use(name, "_ptc", u - 1))
                        for J in range(n + 1):
                            last = pe.transpose(bank[4 + u % 2][:, J * P:(J + 1) * P],
                                                free_x[:, 6 + u % 2, J * P:(J + 1) * P], ident[:])
                    last.then_inc(use(name, "_t")[0], 1)

                def values(u):
                    g, n = units[u]
                    pe.wait_ge(*use(name, "_ptc", u + 1))
                    if u % NT == 0 and g >= 2:
                        pe.wait_ge(*use(name, "_oc", g - 1))
                    for cc in range(2 if dsa else 1):
                        for J in range(n + 1):
                            if dsa:
                                dst = bank[6 + g % 2][HD * cc:HD * cc + HD, n * P:(n + 1) * P]
                                v = v2[:, J, (2 * g + cc) * HD:(2 * g + cc + 1) * HD]
                            else:
                                dst, v = bank[6 + g % 2][:, n * P:(n + 1) * P], v2[:, J, g * P:(g + 1) * P]
                            last = mm(dst, v, free_x[:, 8 + 2 * (u % 2) + cc, J * P:(J + 1) * P], J == 0, J == n)
                    last.then_inc(use(name, "_pv")[0], 1)

                scores(0)
                scores(1)
                for u in range(len(units)):
                    if u + 2 < len(units):
                        scores(u + 2)
                    transposes(u)
                    if u >= 1:
                        values(u - 1)
                values(len(units) - 1)

            pe.wait_ge(sem("evac"), c + 12)
            pe.wait_ge(*use("dq", "_out", 16))
            pairs_attention("a2", False)
            gn_stats("sub")
            gn_apply("sub", None)
            wout("wout2", {k: [use("sub", "_out", k + 1)] for k in range(KT)})
            ffn("mlp0", GROUPS2, 5, False)

            c = at["dsa"]
            def qi_rotate(i):
                if i >= 2:
                    pe.wait_ge(*use("qi", "_sin", i - 1))
                else:
                    pe.wait_ge(*use("kx", "_out", 1))
                    pe.wait_ge(sem("evac"), c + 6)
                mm(bank[4 + i % 2], rot[:, 1, :], qi[:, i, :]).then_inc(use("qi", "_rot")[0], 1)

            def dots(n, heads):
                for hh in heads:
                    u = 8 * (n - 1) + hh
                    if u == 0:
                        pe.wait_ge(*use("qi", "_out", 4))
                        pe.wait_ge(sem("kswap"), 48)
                    if u >= 2:
                        pe.wait_ge(sem("dot_relu"), u - 1)
                    hs = slice(HD * (hh % 2), HD * (hh % 2) + HD)
                    mm(bank[6 + u % 2][:, 0:(n + 1) * P], qi[hs, hh // 2, n * P:(n + 1) * P],
                       ki[hs, 0:(n + 1) * P]).then_inc(sem("dots"), 1)

            blk(c, waits=xg_waits(6))
            stats(6)
            blk(c + 1, ms=(0,))
            gn_stats("cq")
            blk(c + 2)
            pe.wait_ge(sem("evac"), c + 2)
            for n in range(NT):
                last = pe.transpose(bank[6][:, n * P:(n + 1) * P], kw[:, n * P:(n + 1) * P], ident[:])
            last.then_inc(sem("widx_t"), 1)

            def cq_norm(k):
                if k == 4:
                    pe.wait_ge(sem("widx_read"), 1)
                    gn_apply("cq", None)

            def kx_norm(k):
                if k == 4:
                    gn_step("kx", 1, 0)
                if k == 5:
                    rotate("kx", 1, 0)
                if k == 7:
                    qi_rotate(0)
                    qi_rotate(1)

            def first_dots(k):
                if k < 2:
                    qi_rotate(2 + k)
                elif k >= 4:
                    dots(1, (2 * k - 8, 2 * k - 7))

            uq = dict(a=(cq_hi, cq_lo), nk=2)
            blk(c + 3, after=cq_norm)
            blk(c + 4, waits={0: [use("cq", "_out", 2)]}, **uq)
            gn_stats("kx")
            blk(c + 5, **uq)
            blk(c + 6, after=kx_norm)
            blk(c + 7, after=first_dots)
            for i in range(4):
                blk(c + 8 + i, **uq)
                gn_stats("sq", (range(0, 4), range(4, 8), range(8, 12), range(12, 14))[i])
            tok_blk(c + 12, after=lambda t: gn_stats("sq", (14, 15)) if t == 0 else dots(2, range(3 * t - 3, min(8, 3 * t))))
            tok_blk(c + 13, after=lambda t: dots(3, range(2 * t, 2 * t + 2)))
            pe.wait_ge(sem("dot_relu"), 24)
            for i in range(2):
                tok_blk(c + 14 + i, after=lambda t: gn_step("sq", 1, 4 * i + t))
            gn_apply("sq", 1, first=8)
            pe.wait_ge(*use("sq", "_out", 16))
            pe.wait_ge(sem("kmask_done"), 3)
            pairs_attention("a3", True)
            wout("wout3", {k: [use("a3", "_oc", k + 1)] for k in range(KT)})
            ffn("mlp1", GROUPS2, 7, False)
            pe.wait_ge(sem("evac"), NB)
            for n in range(NT):
                for b in range(2):
                    u = 2 * n + b
                    if u >= 4:
                        pe.wait_ge(sem("y_copied"), u - 3)
                    for k in range(4):
                        last = pe.transpose(bank[4 + u % 4][:, k * P:(k + 1) * P], x_res[:, 4 * b + k, n * P:(n + 1) * P], ident[:])
                    last.then_inc(sem("y_tr"), 1)

        @block.scalar
        def _(act):
            def a(out_, in_, f, **kw):
                return act.activation(out_, in_, f, **kw)

            def fin(p, t):
                a(xg_hi[:, t, :], x_res[:, t, :], ACT.Copy, scale=ngain(p, t)).then_inc(sem("xg_hi_done"), 1)
                if t >= 2:
                    act.wait_ge(sem("ssq_done"), 7 * p + max(1, t - 2))
                a(sq[:, t % 2, :], x_res[:, t, :], ACT.Square).then_inc(sem("sq_done"), 1)

            def stats(p):
                act.wait_ge(sem("ms"), p + 1)
                last = a(rstd[:], bank[4], ACT.Sqrt, bias=eps[:])
                if p in (1, 4, 6):
                    last = a(rstd_tok[:], bank[5][:, 0:NT], ACT.Sqrt, bias=eps[:])
                last.then_inc(sem("rms"), 1)

            hcount, scount = [0], [0]

            def ffn(name, groups, p, gated, p_next, between=None):
                stats(p)
                for g, tiles in enumerate(groups):
                    c, h0, s0 = at[name, g, "up"], hcount[0], scount[0]
                    hcount[0] += tiles // 2
                    if gated:
                        scount[0] += tiles // 2
                        with act.Fori(0, tiles // 2) as j:
                            act.wait_ge(sem("evac"), 2 * j + (c + 1))
                            a(buf_c[:], buf_a[:], ACT.Silu).then_inc(sem("silu"), 1)
                            hi(act, c + 2, j)
                            act.wait_ge(sem("hmul"), j + (h0 + 1))
                            a(h_hi[:, bass.ds(2 * j, 2), :], buf_d[:], ACT.Copy).then_inc(sem("h_hi_done"), 1)
                            hi(act, c + 3, j)
                    else:
                        with act.Fori(0, tiles // 4) as j:
                            for s_ in range(2):
                                act.wait_ge(sem("hmul"), 2 * j + (h0 + s_ + 1))
                                a(h_hi[:, bass.ds(4 * j + 2 * s_, 2), :], buf_d[:], ACT.Copy).then_inc(sem("h_hi_done"), 1)
                                hi(act, c + 2 + s_, j)
                    c = at[name, g, "down"]
                    for i in range(4):
                        if g == len(groups) - 1 and p_next is not None:
                            act.wait_ge(sem("evac"), c + i + 1)
                            fin(p_next, 2 * i)
                            fin(p_next, 2 * i + 1)
                        hi(act, c + 2 + i)
                    if between and g == 0:
                        between()

            def gn_squares(name, part):
                for i in part:
                    if i >= 2:
                        act.wait_ge(*use(name, "_msq", i - 1))
                    a(sq[:, i % 2, :], GN[name]["tiles"][i][0], ACT.Square).then_inc(use(name, "_sq")[0], 1)

            def gn_stats(name):
                gn_squares(name, range(len(GN[name]["tiles"])))
                gn_rms(name)

            def gn_rms(name):
                d = GN[name]
                act.wait_ge(*use(name, "_msq", len(d["tiles"])))
                for grp in range(len(d["sizes"])):
                    last = a(rs16[grp], bank[4 + grp][0:16, :], ACT.Sqrt, bias=eps[0:16, :])
                last.then_inc(use(name, "_rms")[0], 1)

            def gn_split(name, dst, src, ready):
                for i, (z, o, grp, idx, g) in enumerate(GN[name]["tiles"]):
                    act.wait_ge(*use(name, ready, i + 1))
                    a(dst[:, o, :], src[:, i % 2, :], ACT.Copy).then_inc(use(name, "_hi")[0], 1)

            def tables(k):
                act.wait_ge(sem("angles"), k + 1)
                a(sin_t[:], sin_t[:], ACT.Sin)
                a(cos_t[:], cos_t[:], ACT.Sin).then_inc(sem("tables"), 1)

            def setup():
                act.wait_ge(sem("lam_mm"), 1)
                a(sm[:, 74:76], bank[6][:, 0:2], ACT.Exp).then_inc(sem("lam_exp"), 1)
                tables(0)

            act.wait_ge(sem("memsets"), 1)
            hi(act, 0)
            act.wait_ge(sem("gains_c"), 1)
            for t in range(KT):
                act.wait_ge(sem("x_copied"), t + 1)
                fin(0, t)
            hi(act, 1)
            ffn("ffn1", GROUPS1, 0, True, 1, between=setup)

            c = at["mix"]
            stats(1)
            for i in range(10):
                hi(act, c + 2 + i)
                if i < 3:
                    act.wait_ge(sem("evac"), c + i + 1)
                    gn_squares("gq", ((0, 1), (2, 3), (4,))[i])
                if i == 4:
                    act.wait_ge(sem("gate_mm"), 2)
                    gn_rms("gq")
                    act.wait_ge(sem("gate_abs"), 1)
                    a(buf_c[:], buf_c[:], ACT.Exp, scale=-1.0).then_inc(sem("gate_exp"), 1)
                    act.wait_ge(sem("gate_exp"), 1)
                    a(buf_c[:], buf_c[:], ACT.Ln, bias=one[:]).then_inc(sem("gate_ln"), 1)

            def gog_silu(m):
                act.wait_ge(sem("evac"), c + 9 + m)
                a(gog[:, 2 * m:2 * m + 2, :], gog[:, 2 * m:2 * m + 2, :], ACT.Silu).then_inc(sem("gog_silu"), 1)

            def a1_exp(h):
                so = 16 * (h % 2)
                act.wait_ge(sem("a1_m"), h + 1)
                if h >= 3:
                    act.wait_ge(sem("a1_t"), h - 2)
                for n in range(NT):
                    a(free_x[:, 2 * (h % 3) + n // 2, (n % 2) * 256:(n % 2 + 1) * 256],
                      bank[2 * (h % 2) + n // 2][:, (n % 2) * 256:(n % 2 + 1) * 256], ACT.Exp,
                      bias=sm[:, so + 4 + n:so + 5 + n], accum_out=sm[:, so + 8 + n:so + 9 + n])
                a(sm[:, so + 12:so + 16], sm[:, so + 4:so + 8], ACT.Exp,
                  bias=sinks[:, h:h + 1]).then_inc(sem("a1_exp"), 1)

            def a1_ptc(h):
                act.wait_ge(sem("a1_t"), h + 1)
                if h >= 2:
                    act.wait_ge(sem("a1_pv"), h - 1)
                a(free_x[:, 6 + 2 * (h % 2):8 + 2 * (h % 2), :], psum[:, 4:6, :], ACT.Copy).then_inc(sem("a1_ptc"), 1)

            def a1_hi(t):
                act.wait_ge(sem("a1_pv"), 2 * t + 2)
                a(h_hi[:, t, :], bank[6 + t % 2], ACT.Copy).then_inc(sem("a1_hi"), 1)

            a1_exp(0)
            a1_exp(1)
            for h in range(8):
                a1_ptc(h)
                if h < 6:
                    a1_exp(h + 2)
                if h % 2 == 0 and h >= 2:
                    a1_hi(h // 2 - 1)
            a1_hi(3)
            gog_silu(0)
            gog_silu(1)

            for i in range(len(LEVELS)):
                act.wait_ge(sem("gla_d"), i + 1)
                a(dl[i % 2], dl[i % 2], ACT.Exp, scale=1 / 16).then_inc(sem("gla_e"), 1)
            act.wait_ge(sem("gla_d"), 8)
            a(dl[1], dl[1], ACT.Exp, scale=1 / 16).then_inc(sem("gla_e"), 1)
            act.wait_ge(sem("gla_q"), 7)
            act.wait_ge(sem("gla_k"), 7)
            a(dl[0], cum.rearrange("p (m t) -> p m t", t=S), ACT.Exp, scale=1 / 16).then_inc(sem("gla_e"), 1)
            act.wait_ge(sem("gla_d"), 9)
            a(dl[1][:, :, 256:512], dl[1][:, :, 256:512], ACT.Exp, scale=1 / 16).then_inc(sem("gla_e"), 1)
            act.wait_ge(sem("gla_d"), 10)
            a(dl[0][:, :, 384:512], dl[0][:, :, 384:512], ACT.Exp, scale=1 / 16).then_inc(sem("gla_e"), 1)
            at0 = 0
            for dq in (1, 2, 3):
                w = NT - dq
                act.wait_ge(sem("gla_x"), dq)
                bk = 4 * ((dq - 1) % 2)
                a(cross_at[:, at0:at0 + 4 * w, :].rearrange("p (h j) i -> p h (j i)", h=4),
                  psum[:, bk:bk + 4, 0:w * P], ACT.Copy).then_inc(sem("gla_xc"), 1)
                at0 += 4 * w
            act.wait_ge(sem("gla_oc"), 4)
            gn_stats("gla")
            gn_split("gla", h_hi, buf_b, "_pre")

            def wout(name, p):
                c = at[name]
                for i in range(4):
                    act.wait_ge(sem("evac"), c + i + 1)
                    fin(p, 2 * i)
                    fin(p, 2 * i + 1)
                    hi(act, c + 2 + i)

            wout("wout1", 2)
            ffn("ffn2", GROUPS1, 2, True, 3)

            act.wait_ge(sem("p_tr"), 2)
            a(h_hi[:, 0:2, :], psum[:, 6:8, :], ACT.Copy).then_inc(sem("p_hi"), 1)
            c = at["proj"]
            act.wait_ge(sem("ssq_done"), 28)
            for i in range(4):
                act.wait_ge(sem("evac"), c + i + 1)
                for t in (2 * i, 2 * i + 1):
                    if t >= 2:
                        act.wait_ge(sem("emb_ssq"), max(1, t - 2))
                    a(sq[:, t % 2, :], emb[:, t, :], ACT.Square).then_inc(sem("emb_sq"), 1)
                hi(act, c + 2 + i)
            stats(3)
            act.wait_ge(sem("emb_ms"), 1)
            a(buf_c[:, 1, :], bank[5], ACT.Sqrt, bias=eps[:]).then_inc(sem("emb_rms"), 1)
            c = at["gate"]
            for i in range(4):
                act.wait_ge(sem("evac"), c + i + 1)
                a(sig[:, 2 * i:2 * i + 2, :], buf_a[:], ACT.Sigmoid).then_inc(sem("sig"), 1)
                if i < 3:
                    hi(act, c + 2 + i)
            for t in range(KT):
                act.wait_ge(sem("ple_x"), t + 1)
                if t == 0:
                    act.wait_ge(sem("evac"), c + 4)
                fin(4, t)
            hi(act, c + 5)

            c = at["diff"]
            stats(4)
            for i in range(12):
                hi(act, c + 2 + i)
                if i < 8:
                    act.wait_ge(sem("evac"), c + i + 1)
                    gn_squares("dq", (2 * i, 2 * i + 1))
                if i == 7:
                    gn_rms("dq")
                if i == 2:
                    tables(1)

            def pairs_attention(name, dsa):
                units = PAIR_UNITS

                def exp(u):
                    w, so = (units[u][1] + 1) * P, 8 * (u % 4)
                    act.wait_ge(*use(name, "_m", u + 1))
                    if u >= 3:
                        act.wait_ge(*use(name, "_t", u - 2))
                    for cc in range(2):
                        last = a(free_x[:, 2 * (u % 3) + cc, 0:w], bank[2 * (u % 2) + cc][:, 0:w], ACT.Exp,
                                 bias=sm[:, so + cc:so + cc + 1], accum_out=sm[:, so + 2 + cc:so + 3 + cc])
                    last.then_inc(use(name, "_exp")[0], 1)

                def ptc(u):
                    w = (units[u][1] + 1) * P
                    act.wait_ge(*use(name, "_t", u + 1))
                    if u >= 2:
                        act.wait_ge(*use(name, "_pv", u - 1))
                    if dsa:
                        last = a(free_x[:, 8 + 2 * (u % 2):10 + 2 * (u % 2), 0:w], psum[:, 4:6, 0:w], ACT.Copy)
                    else:
                        last = a(free_x[:, 8 + 2 * (u % 2), 0:w], bank[4 + u % 2][:, 0:w], ACT.Copy)
                    last.then_inc(use(name, "_ptc")[0], 1)

                def out_tile(g):
                    act.wait_ge(*use(name, "_pv", 4 * (g + 1)))
                    if dsa:
                        a(h_hi[:, g, :], bank[6 + g % 2], ACT.Copy).then_inc(use(name, "_hi")[0], 1)
                    else:
                        a(q2[:, g, :], bank[6 + g % 2], ACT.Copy).then_inc(use(name, "_oc")[0], 1)

                exp(0)
                exp(1)
                for u, (g, n) in enumerate(units):
                    ptc(u)
                    if u + 2 < len(units):
                        exp(u + 2)
                    if u % NT == 1 and g >= 1:
                        out_tile(g - 1)
                out_tile(KT - 1)

            pairs_attention("a2", False)
            act.wait_ge(*use("a2", "_oc", 8))
            gn_stats("sub")
            gn_split("sub", h_hi, buf_a, "_nrm")
            wout("wout2", 5)
            ffn("mlp0", GROUPS2, 5, False, 6)

            c = at["dsa"]
            stats(6)

            def relus(n):
                for hh in range(8):
                    u, w = 8 * (n - 1) + hh, (n + 1) * P
                    act.wait_ge(sem("dots"), u + 1)
                    if u >= 2:
                        act.wait_ge(sem("dot_acc"), u - 1)
                    a(buf_c[:, u % 2, 0:w], bank[6 + u % 2][:, 0:w], ACT.Relu).then_inc(sem("dot_relu"), 1)

            for i in range(16):
                hi(act, c + 2 + i)
                if i == 0:
                    act.wait_ge(sem("evac"), c + 1)
                    gn_squares("cq", range(2))
                if i == 1:
                    gn_rms("cq")
                if i == 2:
                    gn_split("cq", cq_hi, buf_a, "_nrm")
                    gn_squares("kx", range(1))
                if i == 4:
                    gn_rms("kx")
                if i == 6:
                    relus(1)
                if i == 7:
                    act.wait_ge(sem("evac"), c + 8)
                    gn_squares("sq", range(0, 2))
                if i == 8:
                    gn_squares("sq", range(2, 6))
                if i == 9:
                    act.wait_ge(sem("evac"), c + 9)
                    gn_squares("sq", range(6, 10))
                if i == 10:
                    act.wait_ge(sem("evac"), c + 10)
                    gn_squares("sq", range(10, 12))
                    act.wait_ge(sem("evac"), c + 11)
                    gn_squares("sq", range(12, 14))
                if i == 11:
                    act.wait_ge(sem("evac"), c + 12)
                    gn_squares("sq", range(14, 16))
                    gn_rms("sq")
                    relus(2)
                if i == 12:
                    relus(3)
            pairs_attention("a3", True)
            wout("wout3", 7)
            ffn("mlp1", GROUPS2, 7, False, None)
            for u in range(1, 2 * NT, 2):
                act.wait_ge(sem("y_tr"), u + 1)
                n, b = u // 2, u % 2
                act.wait_ge(sem("y_copied"), u)
                a(arena[:, n * D + b * S:n * D + b * S + S], bank[4 + u % 4], ACT.Copy).then_inc(sem("y_copied"), 1)

        @block.vector
        def _(dve):
            chain = [0]

            def link(ins):
                chain[0] += 1
                ins.then_inc(sem("dve_chain"), 1)
                dve.wait_ge(sem("dve_chain"), chain[0])

            def tt(o, x, y, op):
                return dve.tensor_tensor(o, x, y, op)

            def stt(o, x, s_, y, op0, op1):
                return dve.scalar_tensor_tensor(out=o, in0=x, scalar=s_, in1=y, op0=op0, op1=op1)

            def ts(o, x, s1, s2, op0, op1=None):
                if op1 is None:
                    return dve.tensor_scalar(o, x, s1, None, op0)
                return dve.tensor_scalar(o, x, s1, s2, op0, op1)

            def fin(p, t):
                dve.wait_ge(sem("xg_hi_done"), 8 * p + t + 1)
                stt(xg_lo[:, t, :], x_res[:, t, :], ngain(p, t), xg_hi[:, t, :].bitcast(F32),
                    ALU.mult, ALU.subtract).then_inc(sem("xg_done"), 1)

            def stats(p):
                dve.wait_ge(sem("rms"), p + 1)
                link(dve.reciprocal(rstd[:], rstd[:]))
                if p in (1, 4, 6):
                    link(dve.reciprocal(rstd_tok[:], rstd_tok[:]))

            def evac_scaled(c, dst, j=0, ms=(0, 1)):
                dve.wait_ge(sem("pe_blk"), 2 * j + (c + 1))
                for m in ms:
                    last = tt(dst[:, m, :], two(c, m), rstd[:], ALU.mult)
                last.then_inc(sem("evac"), 1)

            def evac_tok(c, dst, f0):
                dve.wait_ge(sem("pe_blk"), c + 1)
                for t in range(NT):
                    last = ts(dst[:, t, f0:f0 + BC], two(c, t // 2)[:, (t % 2) * BC:(t % 2 + 1) * BC],
                              rstd_tok[:, t:t + 1], None, ALU.mult)
                last.then_inc(sem("evac"), 1)

            def residual(c, i, scale, p_next):
                dve.wait_ge(sem("pe_blk"), c + i + 1)
                for m in range(2):
                    t = 2 * i + m
                    last = stt(x_res[:, t, :], two(c + i, m), scale, x_res[:, t, :], ALU.mult, ALU.add)
                last.then_inc(sem("evac"), 1)
                if p_next is not None:
                    fin(p_next, 2 * i)
                    fin(p_next, 2 * i + 1)
                lo(dve, c + 2 + i)

            hcount, scount = [0], [0]

            def ffn(name, groups, p, gated, scale, p_next, between=None):
                stats(p)
                for g, tiles in enumerate(groups):
                    c, h0, s0 = at[name, g, "up"], hcount[0], scount[0]
                    hcount[0] += tiles // 2
                    if gated:
                        scount[0] += tiles // 2
                        with dve.Fori(0, tiles // 2) as j:
                            evac_scaled(c, buf_a, j)
                            lo(dve, c + 2, j)
                            evac_scaled(c + 1, buf_b, j)
                            dve.wait_ge(sem("evac"), 2 * j + (c + 2))
                            dve.wait_ge(sem("silu"), j + (s0 + 1))
                            tt(buf_d[:], buf_b[:], buf_c[:], ALU.mult).then_inc(sem("hmul"), 1)
                            dve.wait_ge(sem("h_hi_done"), j + (h0 + 1))
                            tt(h_lo[:, bass.ds(2 * j, 2), :], buf_d[:], h_hi[:, bass.ds(2 * j, 2), :].bitcast(F32),
                               ALU.subtract).then_inc(sem("h_done"), 1)
                            lo(dve, c + 3, j)
                    else:
                        with dve.Fori(0, tiles // 4) as j:
                            for s_ in range(2):
                                evac_scaled(c + s_, buf_b, j)
                                dve.wait_ge(sem("evac"), 2 * j + (c + s_ + 1))
                                stt(buf_d[:], buf_b[:], 0.0, buf_b[:], ALU.max, ALU.mult).then_inc(sem("hmul"), 1)
                                dve.wait_ge(sem("h_hi_done"), 2 * j + (h0 + s_ + 1))
                                ht = bass.ds(4 * j + 2 * s_, 2)
                                tt(h_lo[:, ht, :], buf_d[:], h_hi[:, ht, :].bitcast(F32),
                                   ALU.subtract).then_inc(sem("h_done"), 1)
                                lo(dve, c + 2 + s_, j)
                    c = at[name, g, "down"]
                    for i in range(4):
                        residual(c, i, scale, p_next if g == len(groups) - 1 else None)
                    if between and g == 0:
                        between()

            def gn_rsqrt(name):
                dve.wait_ge(*use(name, "_rms", 1))
                for grp in range(len(GN[name]["sizes"])):
                    link(dve.memset(sq[:, grp, :], 0.0))
                    link(dve.reciprocal(sq[0:16, grp, :], rs16[grp]))
                    link(dve.tensor_copy(rs_hi[grp][:], sq[:, grp, :]))
                    last = tt(rs_lo[grp][:], sq[:, grp, :], rs_hi[grp][:].bitcast(F32), ALU.subtract)
                last.then_inc(use(name, "_rs")[0], 1)

            def gn_scale(name, i):
                z, o, grp, idx, g = GN[name]["tiles"][i]
                dve.wait_ge(*use(name, "_bc", i + 1))
                if name == "sq" and i >= 2:
                    dve.wait_ge(*use(name, "_cos", i - 1))
                if g is None:
                    ins = tt(buf_a[:, i % 2, :], bank[6 + i % 2], z, ALU.mult)
                else:
                    ins = stt(buf_a[:, i % 2, :], bank[6 + i % 2], g, z, ALU.mult, ALU.mult)
                ins.then_inc(use(name, "_nrm")[0], 1)

            def rope_out(name, i, o):
                dve.wait_ge(*use(name, "_rot", i + 1))
                if name == "sq" and i >= 2:
                    dve.wait_ge(*use(name, "_out", i - 1))
                tt(buf_b[:, i % 2, :], bank[4 + i % 2], sin_t[:], ALU.mult).then_inc(use(name, "_sin")[0], 1)
                if name == "sq":
                    return
                dve.wait_ge(*use(name, "_sin", i + 1))
                dve.wait_ge(*use(name, "_cos", i + 1))
                tt(o, buf_b[:, i % 2, :], buf_c[:, i % 2, :], ALU.add).then_inc(use(name, "_out")[0], 1)

            def gn_rope(name, part=None):
                tiles = GN[name]["tiles"]
                if part is None:
                    gn_rsqrt(name)
                for i in part or range(len(tiles)):
                    gn_scale(name, i)
                    if i:
                        rope_out(name, i - 1, tiles[i - 1][1])
                    if i == len(tiles) - 1:
                        rope_out(name, i, tiles[i][1])

            def gn_split(name, dhi, dlo, mult=None, rsqrt=True):
                if rsqrt:
                    gn_rsqrt(name)
                for i, (z, o, grp, idx, g) in enumerate(GN[name]["tiles"]):
                    gn_scale(name, i)
                    src = buf_a
                    if mult is not None:
                        dve.wait_ge(*use(name, "_nrm", i + 1))
                        tt(buf_b[:, i % 2, :], buf_a[:, i % 2, :], mult[:, i, :], ALU.mult).then_inc(use(name, "_pre")[0], 1)
                        src = buf_b
                    dve.wait_ge(*use(name, "_hi", i + 1))
                    tt(dlo[:, o, :], src[:, i % 2, :], dhi[:, o, :].bitcast(F32), ALU.subtract).then_inc(use(name, "_out")[0], 1)

            def few_bits(v, bits=8):
                e = math.floor(math.log2(abs(v)))
                q = 2.0 ** (e - bits + 1)
                return math.floor(v / q) * q

            def angles(k):
                dve.wait_ge(sem("pos_mm"), k + 1)
                ang, turns, r = buf_a[:, 0, :], buf_a[:, 1, :], buf_b[:, 0, :]
                link(ts(ang, bank[7], 1024.0, inv[:, k:k + 1], ALU.mult, ALU.mult))
                link(ts(turns, ang, 1 / TWO_PI, ROUND, ALU.mult, ALU.add))
                link(ts(turns, turns, -ROUND, None, ALU.add))
                left, src = TWO_PI, ang
                for _ in range(3):
                    part = few_bits(left)
                    link(stt(r, turns, -part, src, ALU.mult, ALU.add))
                    left, src = left - part, r
                link(stt(r, turns, -left, r, ALU.mult, ALU.add))
                link(ts(sin_t[:], r, 3.1415925, -3.1415925, ALU.min, ALU.max))
                link(stt(cos_t[:], sin_t[:], -1.0, sin_t[:], ALU.mult, ALU.max))
                ts(cos_t[:], cos_t[:], -1.0, math.pi / 2, ALU.mult, ALU.add).then_inc(sem("angles"), 1)

            def setup():
                dve.wait_ge(sem("const_c"), 64)
                dve.wait_ge(sem("const_b"), 16 * 3)
                dve.tensor_copy(spread[:], arena[:, 3072:4096])
                link(dve.tensor_copy(mask_bf[:], arena[:, 0:5 * P]))
                tt(sm[:, 64:65], gains[:, G_LQ:G_LQ + 1], gains[:, G_LK:G_LK + 1], ALU.mult)
                ts(sm[0:8, 66:74], ident[0:8, 0:8], gains[0:8, G_SINK:G_SINK + 1], None, ALU.mult).then_inc(sem("lam_prod"), 1)
                dve.wait_ge(sem("lam_exp"), 1)
                link(ts(sinks, bank[6][:, 8:16], 1024.0, None, ALU.mult))
                link(tt(gcol[:, 4:5], sm[:, 75:76], sm[:, 74:75], ALU.subtract))
                link(ts(gcol[:, 4:5], gcol[:, 4:5], -LAM_INIT, None, ALU.add))
                angles(0)

            dve.memset(buf_d[:, 0, 0:P], 0.0).then_inc(sem("zeroed"), 1)
            dve.memset(mean[:], 1.0 / D)
            dve.memset(one[:], 1.0)
            dve.memset(eps[:], EPS).then_inc(sem("memsets"), 1)
            dve.wait_ge(sem("memsets"), 1)
            dve.wait_ge(sem("gains_t"), 1)
            dve.tensor_copy(gains[:], bank[7][:, 0:G_ROWS]).then_inc(sem("gains_c"), 1)
            dve.wait_ge(sem("gains_c"), 1)
            for i, g in enumerate((G_QN, G_DQ, G_SQ)):
                ts(gcol[:, i:i + 1], gains[:, g:g + 1], HD ** -0.5, None, ALU.mult)
            ts(gcol[:, 3:4], gains[:, G_SUB:G_SUB + 1], 1.0 - LAM_INIT, None, ALU.mult)
            link(dve.tensor_copy(ident_bf[:], ident[:]))
            for t in range(KT):
                dve.wait_ge(sem("x_tr"), t + 1)
                dve.tensor_copy(x_res[:, t, :], bank[4 + t % 3]).then_inc(sem("x_copied"), 1)
                if t:
                    fin(0, t - 1)
                if t == 3:
                    lo(dve, 0)
            fin(0, KT - 1)
            lo(dve, 1)
            ffn("ffn1", GROUPS1, 0, True, 0.5, 1, between=setup)

            c = at["mix"]
            stats(1)
            for i in range(2):
                evac_scaled(c + i, aq[:, 2 * i:2 * i + 2, :])
                lo(dve, c + 2 + i)
            dve.wait_ge(sem("pe_blk"), c + 3)
            tt(ak, two(c + 2, 0), rstd[:], ALU.mult)
            for t in range(NT):
                last = ts(av[:, t, :], two(c + 2, 1)[:, t * P:(t + 1) * P], rstd_tok[:, t:t + 1], None, ALU.mult)
            last.then_inc(sem("evac"), 1)
            lo(dve, c + 4)
            dve.wait_ge(sem("pe_blk"), c + 4)
            tt(glr, two(c + 3, 0)[0:16, :], rstd[0:16, :], ALU.mult).then_inc(sem("evac"), 1)
            lo(dve, c + 5)
            evac_scaled(c + 4, gq)
            lo(dve, c + 6)
            dve.wait_ge(sem("gate_mm"), 2)
            for m in range(2):
                last = ts(buf_a[:, m, :], bank[6 + m], gains[:, G_BG + m:G_BG + m + 1], None, ALU.add)
            last.then_inc(sem("gate_read"), 1)
            dve.wait_ge(sem("gate_read"), 1)
            ts(buf_b[:], buf_a[:], 0.0, None, ALU.min)
            stt(buf_c[:], buf_a[:], -1.0, buf_a[:], ALU.mult, ALU.max).then_inc(sem("gate_abs"), 1)
            gn_rsqrt("gq")
            evac_scaled(c + 5, gk)
            lo(dve, c + 7)
            dve.wait_ge(sem("gate_ln"), 1)
            link(tt(buf_a[:], buf_b[:], buf_c[:], ALU.subtract))
            for m in range(2):
                for t in range(NT):
                    last = dve.tensor_tensor_scan(cum[:, m * S + t * P:m * S + (t + 1) * P], one[:].to_broadcast([P, P]),
                                                  buf_a[:, m, t * P:(t + 1) * P], 0.0, ALU.mult, ALU.add)
            link(last)
            for i in range(2):
                gn_rope("gq", part=(range(0, 4), range(4, 5))[i])
                evac_tok(c + 6 + i, gv, i * BC)
                lo(dve, c + 8 + i)
            for i in range(2):
                evac_scaled(c + 8 + i, gog[:, 2 * i:2 * i + 2, :])
                lo(dve, c + 10 + i)

            def a1_max(h):
                so = 16 * (h % 2)
                dve.wait_ge(sem("a1_s"), h + 1)
                link(dve.tensor_reduce(sm[:, so:so + 4],
                                       psum[:, 2 * (h % 2):2 * (h % 2) + 2, :].rearrange("p a (b k) -> p (a b) k", k=2 * P),
                                       AX.X, ALU.max))
                ts(sm[:, so + 4:so + 8], sm[:, so:so + 4], sinks[:, h:h + 1], -1.0, ALU.max, ALU.mult).then_inc(sem("a1_m"), 1)

            def a1_norm(h):
                so = 16 * (h % 2)
                dve.wait_ge(sem("a1_exp"), h + 1)
                link(tt(sm[:, so + 8:so + 12], sm[:, so + 8:so + 12], sm[:, so + 12:so + 16], ALU.add))
                link(dve.reciprocal(sm[:, so + 8:so + 12], sm[:, so + 8:so + 12]))
                pv = free_x[:, 2 * (h % 3):2 * (h % 3) + 2, :].rearrange("p a (b k) -> p (a b) k", k=2 * P)
                tt(pv, pv, sm[:, so + 8:so + 12].unsqueeze(2).to_broadcast([P, 4, 2 * P]), ALU.mult).then_inc(sem("a1_prob"), 1)

            def a1_lo(t):
                dve.wait_ge(sem("a1_hi"), t + 1)
                tt(h_lo[:, t, :], bank[6 + t % 2], h_hi[:, t, :].bitcast(F32), ALU.subtract).then_inc(sem("a1_out"), 1)

            a1_max(0)
            a1_max(1)
            for h in range(8):
                a1_norm(h)
                if h < 6:
                    a1_max(h + 2)
                if h % 2 == 0 and h >= 2:
                    a1_lo(h // 2 - 1)
            a1_lo(3)

            link(dve.memset(free_x[:, 0:4, :], 0.0))
            dve.wait_ge(sem("mix_const"), 32)
            link(dve.tensor_copy(level[:].rearrange("p a c -> p (a c)"), free_h[:, 12:14, :].rearrange("p a c -> p (a c)")))

            def gla_diff(i):
                s_ = LEVELS[i]
                b = cum.rearrange("p (b w s) -> p b w s", w=2, s=s_)
                d = dl[i % 2].rearrange("p m t -> p (m t)").rearrange("p (b w s) -> p b w s", w=2, s=s_)
                ref = b[:, :, 0, s_ - 1:s_]
                nb_ = 2 * S // (2 * s_)
                if i >= 2:
                    dve.wait_ge(sem("gla_q"), i - 1)
                    dve.wait_ge(sem("gla_k"), i - 1)
                tt(d[:, :, 0, :], ref.to_broadcast([P, nb_, s_]), b[:, :, 0, :], ALU.subtract)
                tt(d[:, :, 1, :], b[:, :, 1, :], ref.to_broadcast([P, nb_, s_]), ALU.subtract).then_inc(sem("gla_d"), 1)

            def gla_keys(i):
                dve.wait_ge(sem("gla_e"), i + 1)
                if i >= 2:
                    dve.wait_ge(sem("gla_s"), i - 1)
                tt(kl[i % 2], gk, dl[i % 2], ALU.mult).then_inc(sem("gla_k"), 1)

            def gla_acc(i):
                dve.wait_ge(sem("gla_s"), i + 1)
                dve.copy_predicated(free_x[:, 0:4, :].rearrange("p a (b q) -> p (a b) q", q=P),
                                    level[:, i:i + 1, :].to_broadcast([P, 16, P]),
                                    psum[:, 4 * (i % 2):4 * (i % 2) + 4, :].rearrange("p a (b q) -> p (a b) q", q=P)
                                    ).then_inc(sem("gla_acc"), 1)

            gla_diff(0)
            nl = len(LEVELS)
            for i in range(nl):
                if i + 1 < nl:
                    gla_diff(i + 1)
                gla_keys(i)
                if i >= 2:
                    dve.wait_ge(sem("gla_acc"), i - 1)
                if i:
                    gla_acc(i - 1)
            cb = cum.rearrange("p (b s) -> p b s", s=P)
            tot = cb[:, :, P - 1:P]
            c4 = cum.rearrange("p (m t s) -> p m t s", t=NT, s=P)
            d1 = dl[1].rearrange("p m (t s) -> p m t s", s=P)
            d0 = dl[0].rearrange("p m (t s) -> p m t s", s=P)
            dve.wait_ge(sem("gla_q"), 6)
            dve.wait_ge(sem("gla_k"), 6)
            tt(dl[1].rearrange("p m (t s) -> p (m t) s", s=P), tot.to_broadcast([P, 2 * NT, P]), cb, ALU.subtract).then_inc(sem("gla_d"), 1)
            dve.wait_ge(sem("gla_acc"), nl - 1)
            gla_acc(nl - 1)
            dve.wait_ge(sem("gla_e"), 8)
            tt(gkx, gk, dl[1], ALU.mult).then_inc(sem("gla_kx"), 1)
            dve.wait_ge(sem("gla_kx"), 1)
            for m in range(2):
                last = tt(d1[:, m, 2:4, :], c4[:, m, 2:4, :], c4[:, m, 1:3, P - 1:P].to_broadcast([P, 2, P]), ALU.add)
            last.then_inc(sem("gla_d"), 1)
            dve.wait_ge(sem("gla_q"), 8)
            for m in range(2):
                last = tt(d0[:, m, 3, :], c4[:, m, 3, :], c4[:, m, 2, P - 1:P].to_broadcast([P, P]), ALU.add)
            link(last)
            for m in range(2):
                last = tt(d0[:, m, 3, :], d0[:, m, 3, :], c4[:, m, 1, P - 1:P].to_broadcast([P, P]), ALU.add)
            last.then_inc(sem("gla_d"), 1)
            dve.wait_ge(sem("gla_acc"), nl)
            gla_acc(nl)
            for h in range(4):
                dve.wait_ge(sem("gla_pv"), h + 1)
                dve.tensor_copy(gla_o[:, h, :], bank[h]).then_inc(sem("gla_oc"), 1)
            dve.wait_ge(sem("gog_silu"), 2)
            gn_split("gla", h_hi, h_lo, gog)
            for i in range(4):
                residual(at["wout1"], i, 1.0, 2)
            ffn("ffn2", GROUPS1, 2, True, 0.5, 3)

            dve.wait_ge(sem("p_hi"), 1)
            dve.tensor_tensor(h_lo[:, 0:2, :], psum[:, 6:8, :], h_hi[:, 0:2, :].bitcast(F32), ALU.subtract).then_inc(sem("p_lo"), 1)
            c = at["proj"]
            for i in range(4):
                dve.wait_ge(sem("pe_blk"), c + i + 1)
                for m in range(2):
                    last = dve.tensor_copy(emb[:, 2 * i + m, :], two(c + i, m))
                last.then_inc(sem("evac"), 1)
                lo(dve, c + 2 + i)
            dve.wait_ge(sem("p_in"), 32)
            dve.tensor_copy(buf_b[0:1, 1, :], arena[0:1, 1024:1536].bitcast(I32)).then_inc(sem("pos_f32"), 1)
            stats(3)
            c = at["gate"]
            for i in range(4):
                evac_scaled(c + i, buf_a)
                if i < 3:
                    lo(dve, c + 2 + i)
                if i == 0:
                    dve.wait_ge(sem("emb_rms"), 1)
                    link(dve.reciprocal(buf_c[:, 1, :], buf_c[:, 1, :]))
                    for t in range(KT):
                        last = stt(emb[:, t, :], emb[:, t, :], gains[:, G_PLE + t:G_PLE + t + 1], buf_c[:, 1, :], ALU.mult, ALU.mult)
                    link(last)
                dve.wait_ge(sem("sig"), i + 1)
                ei, si = emb[:, 2 * i:2 * i + 2, :], sig[:, 2 * i:2 * i + 2, :]
                link(tt(ei, ei, si, ALU.mult))
                for t in (2 * i, 2 * i + 1):
                    tt(x_res[:, t, :], x_res[:, t, :], emb[:, t, :], ALU.add).then_inc(sem("ple_x"), 1)
            for t in range(KT):
                fin(4, t)
            lo(dve, c + 5)

            c = at["diff"]
            stats(4)
            for i in range(4):
                evac_scaled(c + i, q2[:, 2 * i:2 * i + 2, :])
                lo(dve, c + 2 + i)
                if i == 2:
                    angles(1)
            for i in range(4):
                evac_scaled(c + 4 + i, k2[:, 2 * i:2 * i + 2, :])
                lo(dve, c + 6 + i)
            gn_rsqrt("dq")
            dve.wait_ge(sem("tables"), 2)
            for i in range(4):
                evac_tok(c + 8 + i, v2, i * BC)
                lo(dve, c + 10 + i)
                gn_rope("dq", part=range(4 * i, 4 * i + 4))

            def pairs_attention(name, dsa):
                units = PAIR_UNITS

                def smax(u):
                    w, so = (units[u][1] + 1) * P, 8 * (u % 4)
                    dve.wait_ge(*use(name, "_s", u + 1))
                    dve.tensor_reduce(sm[:, so:so + 2], psum[:, 2 * (u % 2):2 * (u % 2) + 2, 0:w], AX.X, ALU.max,
                                      negate=True).then_inc(use(name, "_m")[0], 1)

                def norm(u):
                    w, so = (units[u][1] + 1) * P, 8 * (u % 4)
                    dve.wait_ge(*use(name, "_exp", u + 1))
                    link(dve.reciprocal(sm[:, so + 4:so + 6], sm[:, so + 2:so + 4]))
                    p0, p1 = (free_x[:, 2 * (u % 3) + cc, 0:w] for cc in range(2))
                    if dsa:
                        ts(p0, p0, sm[:, so + 4:so + 5], None, ALU.mult)
                        ts(p1, p1, sm[:, so + 5:so + 6], None, ALU.mult).then_inc(use(name, "_prob")[0], 1)
                    else:
                        d = free_x[:, 6 + u % 2, 0:w]
                        ts(p0, p0, sm[:, so + 4:so + 5], None, ALU.mult)
                        link(tt(sm[:, so + 5:so + 6], sm[:, so + 5:so + 6], gcol[:, 4:5], ALU.mult))
                        if u >= 2:
                            dve.wait_ge(*use(name, "_t", u - 1))
                        stt(d, p1, sm[:, so + 5:so + 6], p0, ALU.mult, ALU.add).then_inc(use(name, "_prob")[0], 1)

                def out_tile(g):
                    dve.wait_ge(*use(name, "_hi", g + 1))
                    tt(h_lo[:, g, :], bank[6 + g % 2], h_hi[:, g, :].bitcast(F32), ALU.subtract).then_inc(use(name, "_oc")[0], 1)

                smax(0)
                smax(1)
                for u, (g, n) in enumerate(units):
                    norm(u)
                    if u + 2 < len(units):
                        smax(u + 2)
                    if dsa and u % NT == 1 and g >= 1:
                        out_tile(g - 1)
                if dsa:
                    out_tile(KT - 1)

            pairs_attention("a2", False)
            gn_split("sub", h_hi, h_lo)
            for i in range(4):
                residual(at["wout2"], i, 1.0, 5)
            ffn("mlp0", GROUPS2, 5, False, 1.0, 6)

            c = at["dsa"]
            stats(6)
            def evac_copy(c, dst):
                dve.wait_ge(sem("pe_blk"), c + 1)
                for m in range(2):
                    last = dve.tensor_copy(dst[:, m, :], two(c, m))
                last.then_inc(sem("evac"), 1)

            def index_sum(n, between=None):
                w = (n + 1) * P
                sc = index_score[n][:, 0:w]
                for hh in range(8):
                    u = 8 * (n - 1) + hh
                    dve.wait_ge(sem("dot_relu"), u + 1)
                    if hh == 0:
                        ts(sc, buf_c[:, u % 2, 0:w], widx[:, n, 0:1], None, ALU.mult).then_inc(sem("dot_acc"), 1)
                    else:
                        dve.wait_ge(sem("dot_acc"), u)
                        stt(sc, buf_c[:, u % 2, 0:w], widx[:, n, hh:hh + 1], sc, ALU.mult, ALU.add).then_inc(sem("dot_acc"), 1)
                    if between:
                        between(hh)
                dve.wait_ge(sem("dot_acc"), 8 * n)
                link(tt(sc[:, n * P:], sc[:, n * P:], chunk_mask, ALU.add))

            def take(n, part):
                sc = index_score[n][:, 0:(n + 1) * P]
                for j in part:
                    turn = (n - 1) * (TOPK // 8) + j + 1
                    dve.max(top8, sc).then_inc(sem("top8"), 1)
                    dve.wait_ge(sem("top8"), turn)
                    dve.match_replace(sc, top8, sc, -3e38).then_inc(sem("taken"), 1)
                    dve.wait_ge(sem("taken"), turn)

            evac_scaled(c, cq)
            lo(dve, c + 2)
            evac_scaled(c + 1, kw.unsqueeze(1), ms=(0,))
            lo(dve, c + 3)
            gn_rsqrt("cq")
            evac_scaled(c + 2, k2[:, 0:2, :])
            lo(dve, c + 4)
            dve.wait_ge(sem("widx_t"), 1)
            dve.tensor_scalar(widx, bank[6].rearrange("p (n f) -> p n f", f=P)[:, :, HD:HD + 8],
                              (8 ** -0.5) * (HD ** -0.5), None, ALU.mult).then_inc(sem("widx_read"), 1)
            gn_split("cq", cq_hi, cq_lo, rsqrt=False)
            evac_scaled(c + 3, k2[:, 2:4, :])
            lo(dve, c + 5)
            for i in range(2):
                evac_copy(c + 4 + i, qi[:, 2 * i:2 * i + 2, :])
                lo(dve, c + 6 + i)
            gn_rope("kx")
            for i in range(4):
                rope_out("qi", i, qi[:, i, :])
                if i == 1:
                    evac_scaled(c + 6, k2[:, 4:6, :])
                    lo(dve, c + 8)
            index_sum(1)
            evac_scaled(c + 7, k2[:, 6:8, :])
            lo(dve, c + 9)
            for i in range(4):
                take(1, range(2 * i, 2 * i + 2))
                evac_copy(c + 8 + i, q2[:, 2 * i:2 * i + 2, :])
                lo(dve, c + 10 + i)
            gn_rsqrt("sq")
            index_sum(2, between=lambda hh: take(1, range(8 + hh, 9 + hh)))
            evac_tok(c + 12, v2, 0)
            lo(dve, c + 14)
            index_sum(3, between=lambda hh: take(2, range(hh, hh + 1)))
            evac_tok(c + 13, v2, BC)
            lo(dve, c + 15)
            for i in range(4):
                gn_rope("sq", part=(i,))
                take(2, range(8 + 2 * i, 10 + 2 * i))
            evac_tok(c + 14, v2, 2 * BC)
            lo(dve, c + 16)
            for i in range(4):
                gn_rope("sq", part=(4 + i,))
                take(3, range(i, i + 1))
            evac_tok(c + 15, v2, 3 * BC)
            lo(dve, c + 17)
            for i in range(8):
                gn_rope("sq", part=(8 + i,))
                take(3, range(4 + 3 * i // 2, 4 + 3 * (i + 1) // 2))
            for n in range(1, NT):
                ts(kmask[:, n - 1, 0:(n + 1) * P], index_score[n][:, 0:(n + 1) * P], -2e38, -BIG, ALU.is_gt,
                   ALU.mult).then_inc(sem("kmask_done"), 1)
            pairs_attention("a3", True)
            for i in range(4):
                residual(at["wout3"], i, 1.0, 7)
            ffn("mlp1", GROUPS2, 7, False, 1.0, None)
            for u in range(0, 2 * NT, 2):
                dve.wait_ge(sem("y_tr"), u + 1)
                if u:
                    dve.wait_ge(sem("y_copied"), u)
                n = u // 2
                dve.tensor_copy(arena[:, n * D:n * D + S], bank[4 + u % 4]).then_inc(sem("y_copied"), 1)

        @block.gpsimd
        def _(pool):
            def add_squares(ready, done, r0, d0, dst):
                for t in range(1, KT):
                    pool.wait_ge(sem(ready), r0 + t + 1)
                    if t == 1:
                        ins = pool.tensor_tensor(dst, sq[:, 0, :], sq[:, 1, :], ALU.add)
                    else:
                        pool.wait_ge(sem(done), d0 + t - 1)
                        ins = pool.tensor_tensor(dst, dst, sq[:, t % 2, :], ALU.add)
                    ins.then_inc(sem(done), 1)

            def fin(p):
                add_squares("sq_done", "ssq_done", 8 * p, 7 * p, ssq[:])

            def rope_cos(name, srcs, ready):
                for i, src in enumerate(srcs):
                    if ready:
                        pool.wait_ge(*use(name, ready, i + 1))
                    if i >= 2:
                        pool.wait_ge(*use(name, "_out", i - 1))
                    pool.tensor_tensor(buf_c[:, i % 2, :], src, cos_t[:], ALU.mult).then_inc(use(name, "_cos")[0], 1)

            def sq_rope():
                def add(i):
                    pool.wait_ge(*use("sq", "_sin", i + 1))
                    pool.wait_ge(*use("sq", "_cos", i + 1))
                    pool.tensor_tensor(GN["sq"]["tiles"][i][1], buf_b[:, i % 2, :], buf_c[:, i % 2, :],
                                       ALU.add).then_inc(use("sq", "_out")[0], 1)

                for i in range(16):
                    pool.wait_ge(*use("sq", "_nrm", i + 1))
                    if i >= 2:
                        pool.wait_ge(*use("sq", "_out", i - 1))
                    pool.tensor_tensor(buf_c[:, i % 2, :], buf_a[:, i % 2, :], cos_t[:],
                                       ALU.mult).then_inc(use("sq", "_cos")[0], 1)
                    if i:
                        add(i - 1)
                add(15)

            def gn_cos(name):
                rope_cos(name, [buf_a[:, i % 2, :] for i in range(len(GN[name]["tiles"]))], "_nrm")

            def gla_q(i, src, dst, part=slice(0, S), e=None, s_=None):
                pool.wait_ge(sem("gla_e"), e)
                if s_:
                    pool.wait_ge(sem("gla_s"), s_)
                pool.tensor_tensor(dst[:, :, part], gq[:, :, part], src[:, :, part], ALU.mult).then_inc(sem("gla_q"), 1)

            fin(0)
            fin(1)
            pool.wait_ge(sem("tables"), 1)
            gn_cos("gq")
            for i in range(len(LEVELS)):
                gla_q(i, dl[i % 2], ql[i % 2], e=i + 1, s_=max(0, i - 1))
            gla_q(7, dl[0], ql[0], e=9, s_=7)
            gla_q(8, dl[1], ql[1], part=slice(256, 512), e=10, s_=6)
            gla_q(9, dl[0], dl[0], part=slice(384, 512), e=11)
            fin(2)
            fin(3)
            add_squares("emb_sq", "emb_ssq", 0, 0, buf_c[:, 0, :])
            fin(4)
            pool.wait_ge(sem("tables"), 2)
            gn_cos("dq")
            fin(5)
            fin(6)
            gn_cos("kx")
            pool.wait_ge(*use("kx", "_out", 1))
            pool.wait_ge(sem("evac"), at["dsa"] + 6)
            rope_cos("qi", [qi[:, i, :] for i in range(4)], None)
            sq_rope()
            fin(7)


INPUTS = ["x", "p", "ffn1_norm", "ffn1_w_gate", "ffn1_w_up", "ffn1_w_down", "mix_norm", "w_in", "q_norm", "k_norm",
          "attn_sinks", "gla_w_gate_up", "gla_b_gate", "gla_out_norm", "w_out", "ffn2_norm", "ffn2_w_gate", "ffn2_w_up",
          "ffn2_w_down", "ple_gate_norm", "ple_w_gate", "ple_w_proj", "ple_norm", "positions_2", "norm_mix_2",
          "norm_mlp_2", "mlp_w1_2", "mlp_w2_2", "diff_w_in_2", "diff_q_norm_2", "diff_k_norm_2", "diff_lam_q1_2",
          "diff_lam_k1_2", "diff_lam_q2_2", "diff_lam_k2_2", "diff_subln_2", "diff_w_out_2", "dsa_w_in_2",
          "dsa_cq_norm_2", "dsa_w_uq_2", "dsa_w_uq_idx_2", "dsa_q_norm_2", "dsa_k_norm_2", "dsa_w_out_2"]


def kernel(**inputs):
    import concourse.bacc as bacc
    from concourse.bass_utils import run_bass_kernel_spmd

    nc = bacc.Bacc("TRN2", target_bir_lowering=False, num_devices=1)
    arrays, io = {}, {}
    given = {name: np.ascontiguousarray(inputs[name]) for name in INPUTS}
    for name, a in {**given, **constants()}.items():
        arrays["in_" + name] = a
        io[name] = nc.dram_tensor("in_" + name, a.shape, mybir.dt.from_np(a.dtype), kind="ExternalInput").ap()
    out = nc.dram_tensor("out_0", (1, S, D), F32, kind="ExternalOutput").ap()
    program(nc, io, out)
    r = run_bass_kernel_spmd(nc, [arrays], core_ids=[0])
    return r.results[0]["out_0"]
```
